# Optimizing a Trainium2 kernel written in Bass

```python
import math
import jax, jax.numpy as jnp
from jax import lax
import numpy as np
import jax
import jax.numpy as jnp

D_MODEL = 1024
BATCH = 1
SEQ = 256
DEPTH = 2

HEAD_DIM = 64
N_MIXERS = 2
DSW_GROUPS = ((128, 1), (512, 4), (2048, 16))
DSW_N_GROUPS = len(DSW_GROUPS)
DSW_HEADS_PER_GROUP = D_MODEL // (2 * HEAD_DIM)
DSW_HEADS = DSW_N_GROUPS * DSW_HEADS_PER_GROUP
DSW_OUT_WIDTH = DSW_HEADS_PER_GROUP * HEAD_DIM
MOBA_HEADS = D_MODEL // HEAD_DIM
MOBA_BLOCK = 256
MOBA_TOPK = 3
MOBA_Q_CHUNK = 32
D_FF = 4 * D_MODEL
REL_BUCKETS = 32
REL_MAX_DISTANCE = 2048
BIAS_HEADS = max(DSW_HEADS, MOBA_HEADS)

N_A_LAYERS = (DEPTH + 1) // 2
N_B_LAYERS = DEPTH // 2
EPS = 1e-6
NEG = -1e30
SCALE = HEAD_DIM ** -0.5


def rmsnorm(x, g):
    xf = x.astype(jnp.float32)
    y = xf * lax.rsqrt(jnp.mean(xf * xf, axis=-1, keepdims=True) + EPS)
    return (y * g.astype(jnp.float32)).astype(x.dtype)

def t5_bucket(dist):
    n = jnp.maximum(dist, 0)
    max_exact = REL_BUCKETS // 2
    nf = jnp.maximum(n, 1).astype(jnp.float32)
    large = max_exact + (jnp.log(nf / max_exact) / math.log(REL_MAX_DISTANCE / max_exact)
                         * (REL_BUCKETS - max_exact)).astype(jnp.int32)
    large = jnp.minimum(large, REL_BUCKETS - 1)
    return jnp.where(n < max_exact, n, large)

def softmax_attend(logits, v, eq):
    m = jnp.max(logits, axis=-1, keepdims=True)
    p = jnp.exp(logits - m)
    den = jnp.sum(p, axis=-1, keepdims=True)
    o = jnp.einsum(eq, p / den, v.astype(jnp.float32))
    return o, (m + jnp.log(den))[..., 0]

def dsw_group(q, k, v, rel_bias, col0, window, dilation):
    B, H, S, hd = q.shape
    n = window // dilation
    blk = n
    L = S // dilation
    nb = -(-L // blk)
    Lp = nb * blk

    def to_sub(t):
        t = t.reshape(B, H, L, dilation, hd).transpose(0, 1, 3, 2, 4)
        return jnp.pad(t, ((0, 0), (0, 0), (0, 0), (0, Lp - L), (0, 0)))

    def band(t):
        t = jnp.pad(t, ((0, 0), (0, 0), (0, 0), (blk, 0), (0, 0))).reshape(B, H, dilation, nb + 1, blk, hd)
        return jnp.concatenate([t[:, :, :, :-1], t[:, :, :, 1:]], axis=4)

    qs, ks, vs = to_sub(q), to_sub(k), to_sub(v)
    qb = qs.reshape(B, H, dilation, nb, blk, hd)
    kb, vb = band(ks), band(vs)
    logits = jnp.einsum('bhrnid,bhrnjd->bhrnij', qb, kb, preferred_element_type=jnp.float32) * SCALE

    i = jnp.arange(blk)[:, None]
    j = jnp.arange(2 * blk)[None, :]
    dist = blk + i - j
    in_band = (dist >= 0) & (dist <= n)
    first = (jnp.arange(nb) == 0)[:, None, None] & (j < blk)[None]
    mask = in_band[None] & ~first
    bias = rel_bias[t5_bucket(dist * dilation)][..., col0:col0 + H].transpose(2, 0, 1)
    logits = jnp.where(mask[None, None, None], logits + bias[None, :, None, None], NEG)

    o, lse = softmax_attend(logits, vb, 'bhrnij,bhrnjd->bhrnid')
    o = o.reshape(B, H, dilation, Lp, hd)[:, :, :, :L].transpose(0, 1, 3, 2, 4).reshape(B, H, S, hd)
    lse = lse.reshape(B, H, dilation, Lp)[..., :L].transpose(0, 1, 3, 2).reshape(B, H, S)
    return o, lse

def dsw_mixer(h, w_qkv, q_gain, k_gain, w_o, rel_bias):
    B, S, _ = h.shape
    G, Hg = DSW_N_GROUPS, DSW_HEADS_PER_GROUP
    qkv = (h @ w_qkv).reshape(B, S, 3, G, Hg, HEAD_DIM)
    q = rmsnorm(qkv[:, :, 0], q_gain)
    k = rmsnorm(qkv[:, :, 1], k_gain)
    v = qkv[:, :, 2]
    outs, lses = [], []
    for g, (window, dilation) in enumerate(DSW_GROUPS):
        o, lse = dsw_group(q[:, :, g].transpose(0, 2, 1, 3), k[:, :, g].transpose(0, 2, 1, 3),
                           v[:, :, g].transpose(0, 2, 1, 3), rel_bias, g * Hg, window, dilation)
        outs.append(o)
        lses.append(lse)
    wts = jax.nn.softmax(jnp.stack(lses), axis=0)
    o = jnp.einsum('gbhs,gbhsd->bshd', wts, jnp.stack(outs)).reshape(B, S, DSW_OUT_WIDTH)
    return o.astype(h.dtype) @ w_o

def gather_blocks(blocks, idx):
    return jax.vmap(jax.vmap(lambda bl, ix: bl[ix]))(blocks, idx)

def moba_mixer(h, w_qkv, q_gain, k_gain, w_o, rel_bias):
    B, S, _ = h.shape
    H, hd, blk = MOBA_HEADS, HEAD_DIM, MOBA_BLOCK
    qkv = (h @ w_qkv).reshape(B, S, 3, H, hd)
    q = rmsnorm(qkv[:, :, 0], q_gain).transpose(0, 2, 1, 3)
    k = rmsnorm(qkv[:, :, 1], k_gain).transpose(0, 2, 1, 3)
    v = qkv[:, :, 2].transpose(0, 2, 1, 3)
    nblk = -(-S // blk)
    Sp = nblk * blk
    pad = ((0, 0), (0, 0), (0, Sp - S), (0, 0))
    q, k, v = jnp.pad(q, pad), jnp.pad(k, pad), jnp.pad(v, pad)
    qb = q.reshape(B, H, nblk, blk, hd)
    kb = k.reshape(B, H, nblk, blk, hd)
    vb = v.reshape(B, H, nblk, blk, hd)
    pos = jnp.arange(Sp)
    qblk = pos // blk
    table_h = rel_bias[:, :H].T

    ii = jnp.arange(blk)
    own_bias = table_h[:, t5_bucket(ii[:, None] - ii[None, :])]
    lo = jnp.einsum('bhnid,bhnjd->bhnij', qb, kb, preferred_element_type=jnp.float32) * SCALE
    lo = jnp.where(ii[:, None] >= ii[None, :], lo + own_bias[None, :, None], NEG)
    o_own, lse_own = softmax_attend(lo, vb, 'bhnij,bhnjd->bhnid')
    o_own = o_own.reshape(B, H, Sp, hd)
    lse_own = lse_own.reshape(B, H, Sp)

    kmean = jnp.mean(kb.astype(jnp.float32), axis=3)
    gate = jnp.einsum('bhsd,bhnd->bhsn', q.astype(jnp.float32), kmean)
    past = jnp.arange(nblk)[None, :] < qblk[:, None]
    gate = jnp.where(past, gate, -jnp.inf)
    topk = min(MOBA_TOPK, nblk)
    _, sel = lax.top_k(gate, topk)
    sel_valid = sel < qblk[:, None]

    C = MOBA_Q_CHUNK
    nC = Sp // C

    def chunk(t):
        return jnp.moveaxis(t.reshape(B, H, nC, C, *t.shape[3:]), 2, 0)

    jj = jnp.arange(blk)
    head_ix = jnp.arange(H)[None, :, None, None]

    def attend(args):
        qc, selc, validc, posc = args
        flat = selc.reshape(B, H, C * topk)
        kg = gather_blocks(kb, flat).reshape(B, H, C, topk * blk, hd)
        vg = gather_blocks(vb, flat).reshape(B, H, C, topk * blk, hd)
        logits = jnp.einsum('bhcd,bhckd->bhck', qc, kg, preferred_element_type=jnp.float32) * SCALE
        kpos = (selc[..., None] * blk + jj).reshape(B, H, C, topk * blk)
        bias = table_h[head_ix, t5_bucket(posc[None, None, :, None] - kpos)]
        valid = jnp.repeat(validc, blk, axis=-1)
        logits = jnp.where(valid, logits + bias, NEG)
        return softmax_attend(logits, vg, 'bhck,bhckd->bhcd')

    o_sel, lse_sel = lax.map(attend, (chunk(q), chunk(sel), chunk(sel_valid), pos.reshape(nC, C)))
    o_sel = jnp.moveaxis(o_sel, 0, 2).reshape(B, H, Sp, hd)
    lse_sel = jnp.moveaxis(lse_sel, 0, 2).reshape(B, H, Sp)

    lse = jnp.logaddexp(lse_own, lse_sel)
    o = jnp.exp(lse_own - lse)[..., None] * o_own + jnp.exp(lse_sel - lse)[..., None] * o_sel
    o = o[:, :, :S].transpose(0, 2, 1, 3).reshape(B, S, H * hd)
    return o.astype(h.dtype) @ w_o

def sq_relu_mlp(h, w1, w2):
    return jnp.square(jax.nn.relu(h @ w1)) @ w2

def first_inputs(seed: int = 0) -> dict:
    key = jax.random.key(seed)
    ks = jax.random.split(key, 16)
    D = D_MODEL
    nrm = lambda k, shape, s: jax.random.normal(k, shape, jnp.float32) * s
    a_qkv_cols = 3 * DSW_HEADS * HEAD_DIM
    b_qkv_cols = 3 * MOBA_HEADS * HEAD_DIM
    return {
        "x": nrm(ks[0], (BATCH, SEQ, D), 1.0),
        "rel_bias": nrm(ks[1], (REL_BUCKETS, BIAS_HEADS), 0.3),
        "norm_mix": 1.0 + nrm(ks[2], (DEPTH, D), 0.02),
        "norm_ffn": 1.0 + nrm(ks[3], (DEPTH, D), 0.02),
        "a_w_qkv": nrm(ks[4], (N_A_LAYERS, D, a_qkv_cols), D ** -0.5),
        "a_q_gain": 1.0 + nrm(ks[5], (N_A_LAYERS, HEAD_DIM), 0.02),
        "a_k_gain": 1.0 + nrm(ks[6], (N_A_LAYERS, HEAD_DIM), 0.02),
        "a_w_o": nrm(ks[7], (N_A_LAYERS, DSW_OUT_WIDTH, D), DSW_OUT_WIDTH ** -0.5),
        "b_w_qkv": nrm(ks[8], (N_B_LAYERS, D, b_qkv_cols), D ** -0.5),
        "b_q_gain": 1.0 + nrm(ks[9], (N_B_LAYERS, HEAD_DIM), 0.02),
        "b_k_gain": 1.0 + nrm(ks[10], (N_B_LAYERS, HEAD_DIM), 0.02),
        "b_w_o": nrm(ks[11], (N_B_LAYERS, MOBA_HEADS * HEAD_DIM, D), (MOBA_HEADS * HEAD_DIM) ** -0.5),
        "ffn_w1": nrm(ks[12], (DEPTH, D, D_FF), D ** -0.5),
        "ffn_w2": nrm(ks[13], (DEPTH, D_FF, D), 0.5 * D_FF ** -0.5),
    }

def first_block(x, rel_bias, norm_mix, norm_ffn, a_w_qkv, a_q_gain, a_k_gain, a_w_o,
              b_w_qkv, b_q_gain, b_k_gain, b_w_o, ffn_w1, ffn_w2):
    h = x
    for i in range(DEPTH):
        u = rmsnorm(h, norm_mix[i])
        li = i // N_MIXERS
        if i % N_MIXERS == 0:
            h = h + dsw_mixer(u, a_w_qkv[li], a_q_gain[li], a_k_gain[li], a_w_o[li], rel_bias)
        else:
            h = h + moba_mixer(u, b_w_qkv[li], b_q_gain[li], b_k_gain[li], b_w_o[li], rel_bias)
        h = h + sq_relu_mlp(rmsnorm(h, norm_ffn[i]), ffn_w1[i], ffn_w2[i])
    return h


CTX_LEN = 256
GRID_W = 64
ROPE_THETA = 10000.0
QBLK = 128

A_HEADS = (D_MODEL // 2) // HEAD_DIM
A_KV_HEADS = A_HEADS // 4
A_WIDTH = A_HEADS * HEAD_DIM
B_WIDTH = D_MODEL - A_WIDTH
CONV_WIDTH = 31
AB_IN = A_WIDTH + 2 * A_KV_HEADS * HEAD_DIM + 2 * B_WIDTH

C_HEADS = (D_MODEL // 2) // HEAD_DIM
C_KV_HEADS = C_HEADS // 4
C_WIDTH = C_HEADS * HEAD_DIM
WINDOW = 128
D_WIDTH = D_MODEL - C_WIDTH
POOL_SIZES = (2, 4, 8, 16)
POOL_GROUP_WIDTH = D_WIDTH // len(POOL_SIZES)
CD_IN = C_WIDTH + 2 * C_KV_HEADS * HEAD_DIM + D_WIDTH

N_EXPERT_GROUPS = 4
EXPERTS_PER_GROUP = 8
N_EXPERTS = N_EXPERT_GROUPS * EXPERTS_PER_GROUP
TOP_K_INNER = 2
D_EXPERT = D_MODEL // 2
MOE_BLOCK = 128


def _rmsnorm(x, g):
    xf = x.astype(jnp.float32)
    y = xf * lax.rsqrt(jnp.mean(xf * xf, axis=-1, keepdims=True) + EPS)
    return (y * g.astype(jnp.float32)).astype(x.dtype)

def _modulate(h, shift, scale):
    return h * (1 + scale) + shift

def _rope_tables(n_lat):
    rows = n_lat // GRID_W
    row = jnp.repeat(jnp.arange(rows, dtype=jnp.float32), GRID_W)
    col = jnp.tile(jnp.arange(GRID_W, dtype=jnp.float32), rows)
    n_freq = HEAD_DIM // 4
    inv = ROPE_THETA ** (-jnp.arange(n_freq, dtype=jnp.float32) / n_freq)
    ang = jnp.concatenate([row[:, None] * inv, col[:, None] * inv], axis=-1)
    return jnp.cos(ang), jnp.sin(ang)

def _rope(x, cos, sin):
    half = HEAD_DIM // 2
    x1, x2 = x[..., :half], x[..., half:]
    c = cos.astype(x.dtype)
    s = sin.astype(x.dtype)
    return jnp.concatenate([x1 * c - x2 * s, x2 * c + x1 * s], axis=-1)

def _heads(t, n):
    b, s, _ = t.shape
    return t.reshape(b, s, n, HEAD_DIM).transpose(0, 2, 1, 3)

def _group(q, n_kv):
    b, h, s, d = q.shape
    return q.reshape(b, n_kv, h // n_kv, s, d)

def _merge(o):
    b, k, g, s, d = o.shape
    return o.transpose(0, 3, 1, 2, 4).reshape(b, s, k * g * d)

def _attend(q, k, v, mask, sink):
    s = jnp.einsum('bkgqd,bksd->bkgqs', q, k).astype(jnp.float32) * (HEAD_DIM ** -0.5)
    if mask is not None:
        s = jnp.where(mask, s, -jnp.inf)
    if sink is None:
        p = jax.nn.softmax(s, axis=-1)
    else:
        sk = jnp.broadcast_to(sink.astype(jnp.float32)[None, :, :, None, None], s.shape[:-1] + (1,))
        p = jax.nn.softmax(jnp.concatenate([s, sk], axis=-1), axis=-1)[..., :-1]
    return jnp.einsum('bkgqs,bksd->bkgqd', p.astype(v.dtype), v)

def _dense_attn_blocks(q, k, v):
    b, hk, g, s, d = q.shape
    nb = s // QBLK
    qb = jnp.moveaxis(q.reshape(b, hk, g, nb, QBLK, d), 3, 0)
    ob = lax.map(lambda qi: _attend(qi, k, v, None, None), qb)
    return jnp.moveaxis(ob, 0, 3).reshape(b, hk, g, s, d)

def _window_attn_blocks(q, k_lat, v_lat, k_ctx, v_ctx, sink):
    b, hk, g, s, d = q.shape
    nb = s // QBLK
    span = QBLK + 2 * WINDOW
    n_ctx = k_ctx.shape[2]
    pad = ((0, 0), (0, 0), (WINDOW, WINDOW), (0, 0))
    kp = jnp.pad(k_lat, pad)
    vp = jnp.pad(v_lat, pad)
    qb = jnp.moveaxis(q.reshape(b, hk, g, nb, QBLK, d), 3, 0)
    r = jnp.arange(QBLK)
    j = jnp.arange(span)
    ctx_mask = jnp.ones((QBLK, n_ctx), dtype=bool)

    def block(args):
        qi, i = args
        start = i * QBLK
        kw = lax.dynamic_slice_in_dim(kp, start, span, axis=2)
        vw = lax.dynamic_slice_in_dim(vp, start, span, axis=2)
        qpos = start + r
        kpos = start - WINDOW + j
        band = (jnp.abs(qpos[:, None] - kpos[None, :]) <= WINDOW) & ((kpos >= 0) & (kpos < s))[None, :]
        mask = jnp.concatenate([ctx_mask, band], axis=1)
        return _attend(qi, jnp.concatenate([k_ctx, kw], axis=2), jnp.concatenate([v_ctx, vw], axis=2), mask, sink)

    ob = lax.map(block, (qb, jnp.arange(nb)))
    return jnp.moveaxis(ob, 0, 3).reshape(b, hk, g, s, d)

def _conv_module(u, conv_w, conv_b, ln_g, ln_b):
    a, gate = jnp.split(u, 2, axis=-1)
    glu = a * jax.nn.sigmoid(gate)
    y = lax.conv_general_dilated(glu, conv_w[:, None, :], window_strides=(1,),
                                 padding=[(CONV_WIDTH // 2, CONV_WIDTH // 2)],
                                 dimension_numbers=('NWC', 'WIO', 'NWC'),
                                 feature_group_count=B_WIDTH) + conv_b
    yf = y.astype(jnp.float32)
    mu = jnp.mean(yf, axis=-1, keepdims=True)
    var = jnp.mean((yf - mu) ** 2, axis=-1, keepdims=True)
    yn = ((yf - mu) * lax.rsqrt(var + EPS) * ln_g.astype(jnp.float32) + ln_b.astype(jnp.float32)).astype(u.dtype)
    return jax.nn.silu(yn)

def _pool_mixer(u, pool_w, pool_scale):
    b, s, _ = u.shape
    uf = u.astype(jnp.float32)
    cs = jnp.pad(jnp.cumsum(uf, axis=1), ((0, 0), (1, 0), (0, 0)))
    t = jnp.arange(s)
    outs = []
    for gi, w in enumerate(POOL_SIZES):
        lo_c, hi_c = gi * POOL_GROUP_WIDTH, (gi + 1) * POOL_GROUP_WIDTH
        lo = jnp.clip(t - w // 2, 0, s)
        hi = jnp.clip(t - w // 2 + w, 0, s)
        csg = cs[..., lo_c:hi_c]
        mean = (jnp.take(csg, hi, axis=1) - jnp.take(csg, lo, axis=1)) / (hi - lo).astype(jnp.float32)[None, :, None]
        outs.append(mean - uf[..., lo_c:hi_c])
    p = jnp.stack(outs, axis=2).astype(u.dtype)
    y = jnp.einsum('bsgc,gcd->bsgd', p, pool_w).reshape(b, s, D_WIDTH)
    return y * pool_scale

def _mixer_ab(hx, hc, w_in, w_out, q_g, k_g, conv_w, conv_b, ln_g, ln_b, cos, sin, ctx_out):
    kvw = A_KV_HEADS * HEAD_DIM
    o_k, o_v, o_u = A_WIDTH, A_WIDTH + kvw, A_WIDTH + 2 * kvw
    px = hx @ w_in
    qx = _rope(_rmsnorm(_heads(px[..., :o_k], A_HEADS), q_g), cos, sin)
    kx = _rope(_rmsnorm(_heads(px[..., o_k:o_v], A_KV_HEADS), k_g), cos, sin)
    vx = _heads(px[..., o_v:o_u], A_KV_HEADS)
    if ctx_out:
        pc = hc @ w_in
        kvc = pc[..., o_k:o_u]
    else:
        kvc = hc @ w_in[:, o_k:o_u]
    kc = _rmsnorm(_heads(kvc[..., :kvw], A_KV_HEADS), k_g)
    vc = _heads(kvc[..., kvw:], A_KV_HEADS)
    ox = _dense_attn_blocks(_group(qx, A_KV_HEADS), jnp.concatenate([kc, kx], axis=2), jnp.concatenate([vc, vx], axis=2))
    bx = _conv_module(px[..., o_u:], conv_w, conv_b, ln_g, ln_b)
    yx = jnp.concatenate([_merge(ox), bx], axis=-1) @ w_out
    if not ctx_out:
        return yx, None
    qc = _rmsnorm(_heads(pc[..., :o_k], A_HEADS), q_g)
    oc = _attend(_group(qc, A_KV_HEADS), kc, vc, None, None)
    bc = _conv_module(pc[..., o_u:], conv_w, conv_b, ln_g, ln_b)
    yc = jnp.concatenate([_merge(oc), bc], axis=-1) @ w_out
    return yx, yc

def _mixer_cd(hx, hc, w_in, w_out, q_g, k_g, sink, pool_w, pool_scale, cos, sin, ctx_out):
    kvw = C_KV_HEADS * HEAD_DIM
    o_k, o_v, o_u = C_WIDTH, C_WIDTH + kvw, C_WIDTH + 2 * kvw
    sink_g = sink.reshape(C_KV_HEADS, C_HEADS // C_KV_HEADS)
    px = hx @ w_in
    qx = _rope(_rmsnorm(_heads(px[..., :o_k], C_HEADS), q_g), cos, sin)
    kx = _rope(_rmsnorm(_heads(px[..., o_k:o_v], C_KV_HEADS), k_g), cos, sin)
    vx = _heads(px[..., o_v:o_u], C_KV_HEADS)
    if ctx_out:
        pc = hc @ w_in
        kvc = pc[..., o_k:o_u]
    else:
        kvc = hc @ w_in[:, o_k:o_u]
    kc = _rmsnorm(_heads(kvc[..., :kvw], C_KV_HEADS), k_g)
    vc = _heads(kvc[..., kvw:], C_KV_HEADS)
    ox = _window_attn_blocks(_group(qx, C_KV_HEADS), kx, vx, kc, vc, sink_g)
    dx = _pool_mixer(px[..., o_u:], pool_w, pool_scale)
    yx = jnp.concatenate([_merge(ox), dx], axis=-1) @ w_out
    if not ctx_out:
        return yx, None
    qc = _rmsnorm(_heads(pc[..., :o_k], C_HEADS), q_g)
    oc = _attend(_group(qc, C_KV_HEADS), kc, vc, None, sink_g)
    dc = _pool_mixer(pc[..., o_u:], pool_w, pool_scale)
    yc = jnp.concatenate([_merge(oc), dc], axis=-1) @ w_out
    return yx, yc

def _moe(h, grp_w, grp_b, exp_w, exp_b, w_gate, w_up, w_down):
    n_tok, d = h.shape
    tok_idx = jnp.arange(n_tok)
    g_logits = (h @ grp_w).astype(jnp.float32) + grp_b.astype(jnp.float32)
    g_sel = jnp.argmax(g_logits, axis=-1)
    g_w = jax.nn.softmax(g_logits, axis=-1)[tok_idx, g_sel]
    e_logits = ((h @ exp_w).astype(jnp.float32) + exp_b.astype(jnp.float32)).reshape(n_tok, N_EXPERT_GROUPS, EXPERTS_PER_GROUP)[tok_idx, g_sel]
    e_p, e_i = lax.top_k(jax.nn.softmax(e_logits, axis=-1), TOP_K_INNER)
    wts = (g_w[:, None] * e_p / jnp.sum(e_p, axis=-1, keepdims=True)).reshape(-1)
    eid = (g_sel[:, None] * EXPERTS_PER_GROUP + e_i).reshape(-1).astype(jnp.int32)
    n_asg = n_tok * TOP_K_INNER
    flat_tok = jnp.repeat(tok_idx, TOP_K_INNER).astype(jnp.int32)
    order = jnp.argsort(eid)
    se, stok, sw = eid[order], flat_tok[order], wts[order]
    counts = jnp.bincount(eid, length=N_EXPERTS).astype(jnp.int32)
    padded = (counts + MOE_BLOCK - 1) // MOE_BLOCK * MOE_BLOCK
    start = jnp.cumsum(counts) - counts
    pend = jnp.cumsum(padded)
    dest = (pend - padded)[se] + jnp.arange(n_asg, dtype=jnp.int32) - start[se]
    n_blk = -(-(n_asg + N_EXPERTS * (MOE_BLOCK - 1)) // MOE_BLOCK)
    cap = n_blk * MOE_BLOCK
    buf_tok = jnp.full((cap,), n_tok, jnp.int32).at[dest].set(stok)
    buf_w = jnp.zeros((cap,), h.dtype).at[dest].set(sw.astype(h.dtype))
    blk_e = jnp.minimum(jnp.searchsorted(pend, jnp.arange(n_blk, dtype=jnp.int32) * MOE_BLOCK, side='right'), N_EXPERTS - 1)
    h_pad = jnp.concatenate([h, jnp.zeros((1, d), h.dtype)], axis=0)

    def run(args):
        tok, wt, e = args
        xb = h_pad[tok]
        hid = jax.nn.silu(xb @ w_gate[e]) * (xb @ w_up[e])
        return (hid @ w_down[e]) * wt[:, None]

    ys = lax.map(run, (buf_tok.reshape(n_blk, MOE_BLOCK), buf_w.reshape(n_blk, MOE_BLOCK), blk_e))
    out = jnp.zeros((n_tok + 1, d), h.dtype).at[buf_tok].add(ys.reshape(cap, d))
    return out[:n_tok]

def second_inputs(seed: int = 0) -> dict:
    key = jax.random.key(seed)
    keys = jax.random.split(key, 48)
    counter = iter(range(48))

    def nrm(shape, scale):
        return jax.random.normal(keys[next(counter)], shape, jnp.float32) * scale

    n_even = (DEPTH + 1) // 2
    n_odd = DEPTH // 2
    dm = D_MODEL
    return {
        'x': nrm((BATCH, SEQ, dm), 1.0),
        'c': nrm((BATCH, dm), 1.0),
        'ctx': nrm((BATCH, CTX_LEN, dm), 1.0),
        'c_ctx': nrm((dm,), 1.0),
        'mod_w': nrm((DEPTH, dm, 6 * dm), 0.5 * dm ** -0.5),
        'mod_b': nrm((DEPTH, 6 * dm), 0.02),
        'ln1_g': 1.0 + nrm((DEPTH, dm), 0.02),
        'ln2_g': 1.0 + nrm((DEPTH, dm), 0.02),
        'w_in_ab': nrm((n_even, dm, AB_IN), dm ** -0.5),
        'w_out_ab': nrm((n_even, A_WIDTH + B_WIDTH, dm), dm ** -0.5),
        'q_norm_a': 1.0 + nrm((n_even, HEAD_DIM), 0.02),
        'k_norm_a': 1.0 + nrm((n_even, HEAD_DIM), 0.02),
        'conv_w': nrm((n_even, CONV_WIDTH, B_WIDTH), CONV_WIDTH ** -0.5),
        'conv_b': nrm((n_even, B_WIDTH), 0.02),
        'conv_ln_g': 1.0 + nrm((n_even, B_WIDTH), 0.02),
        'conv_ln_b': nrm((n_even, B_WIDTH), 0.02),
        'w_in_cd': nrm((n_odd, dm, CD_IN), dm ** -0.5),
        'w_out_cd': nrm((n_odd, C_WIDTH + D_WIDTH, dm), dm ** -0.5),
        'q_norm_c': 1.0 + nrm((n_odd, HEAD_DIM), 0.02),
        'k_norm_c': 1.0 + nrm((n_odd, HEAD_DIM), 0.02),
        'sink_c': nrm((n_odd, C_HEADS), 0.5),
        'pool_w': nrm((n_odd, len(POOL_SIZES), POOL_GROUP_WIDTH, POOL_GROUP_WIDTH), POOL_GROUP_WIDTH ** -0.5),
        'pool_scale': 1.0 + nrm((n_odd, D_WIDTH), 0.02),
        'rt_grp_w': nrm((DEPTH, dm, N_EXPERT_GROUPS), dm ** -0.5),
        'rt_grp_b': nrm((DEPTH, N_EXPERT_GROUPS), 0.01),
        'rt_exp_w': nrm((DEPTH, dm, N_EXPERTS), dm ** -0.5),
        'rt_exp_b': nrm((DEPTH, N_EXPERTS), 0.01),
        'ex_gate': nrm((DEPTH, N_EXPERTS, dm, D_EXPERT), dm ** -0.5),
        'ex_up': nrm((DEPTH, N_EXPERTS, dm, D_EXPERT), dm ** -0.5),
        'ex_down': nrm((DEPTH, N_EXPERTS, D_EXPERT, dm), D_EXPERT ** -0.5),
    }

def second_block(x, c, ctx, c_ctx, mod_w, mod_b, ln1_g, ln2_g,
              w_in_ab, w_out_ab, q_norm_a, k_norm_a, conv_w, conv_b, conv_ln_g, conv_ln_b,
              w_in_cd, w_out_cd, q_norm_c, k_norm_c, sink_c, pool_w, pool_scale,
              rt_grp_w, rt_grp_b, rt_exp_w, rt_exp_b, ex_gate, ex_up, ex_down):
    b, s, dm = x.shape
    cos, sin = _rope_tables(s)
    for i in range(DEPTH):
        last = i == DEPTH - 1
        li = i // 2
        mod = jax.nn.silu(c) @ mod_w[i] + mod_b[i]
        modc = jax.nn.silu(c_ctx) @ mod_w[i] + mod_b[i]
        sh1, sc1, g1, sh2, sc2, g2 = jnp.split(mod[:, None, :], 6, axis=-1)
        sh1c, sc1c, g1c, sh2c, sc2c, g2c = jnp.split(modc[None, None, :], 6, axis=-1)
        hx = _modulate(_rmsnorm(x, ln1_g[i]), sh1, sc1)
        hc = _modulate(_rmsnorm(ctx, ln1_g[i]), sh1c, sc1c)
        if i % 2 == 0:
            yx, yc = _mixer_ab(hx, hc, w_in_ab[li], w_out_ab[li], q_norm_a[li], k_norm_a[li],
                               conv_w[li], conv_b[li], conv_ln_g[li], conv_ln_b[li], cos, sin, not last)
        else:
            yx, yc = _mixer_cd(hx, hc, w_in_cd[li], w_out_cd[li], q_norm_c[li], k_norm_c[li],
                               sink_c[li], pool_w[li], pool_scale[li], cos, sin, not last)
        x = x + g1 * yx
        hx = _modulate(_rmsnorm(x, ln2_g[i]), sh2, sc2)
        if last:
            ox = _moe(hx.reshape(b * s, dm), rt_grp_w[i], rt_grp_b[i], rt_exp_w[i], rt_exp_b[i],
                      ex_gate[i], ex_up[i], ex_down[i]).reshape(b, s, dm)
            x = x + g2 * ox
        else:
            ctx = ctx + g1c * yc
            hc = _modulate(_rmsnorm(ctx, ln2_g[i]), sh2c, sc2c)
            n_ctx = ctx.shape[1]
            tokens = jnp.concatenate([hc, hx], axis=1).reshape(-1, dm)
            out = _moe(tokens, rt_grp_w[i], rt_grp_b[i], rt_exp_w[i], rt_exp_b[i],
                       ex_gate[i], ex_up[i], ex_down[i]).reshape(b, n_ctx + s, dm)
            ctx = ctx + g2c * out[:, :n_ctx]
            x = x + g2 * out[:, n_ctx:]
    return x


def setup_inputs(seed=0):
    out = dict(first_inputs(seed))
    for name, value in second_inputs(seed + 1).items():
        if name != "x":
            out[name + "_2"] = value
    return out


def reference(
    x, rel_bias, norm_mix, norm_ffn, a_w_qkv, a_q_gain, a_k_gain, a_w_o, b_w_qkv, b_q_gain,
    b_k_gain, b_w_o, ffn_w1, ffn_w2, c_2, ctx_2, c_ctx_2, mod_w_2, mod_b_2, ln1_g_2, ln2_g_2,
    w_in_ab_2, w_out_ab_2, q_norm_a_2, k_norm_a_2, conv_w_2, conv_b_2, conv_ln_g_2, conv_ln_b_2,
    w_in_cd_2, w_out_cd_2, q_norm_c_2, k_norm_c_2, sink_c_2, pool_w_2, pool_scale_2, rt_grp_w_2,
    rt_grp_b_2, rt_exp_w_2, rt_exp_b_2, ex_gate_2, ex_up_2, ex_down_2,
):
    x = first_block(
        x, rel_bias, norm_mix, norm_ffn, a_w_qkv, a_q_gain, a_k_gain, a_w_o, b_w_qkv, b_q_gain,
        b_k_gain, b_w_o, ffn_w1, ffn_w2,
    )
    return second_block(
        x, c_2, ctx_2, c_ctx_2, mod_w_2, mod_b_2, ln1_g_2, ln2_g_2, w_in_ab_2, w_out_ab_2,
        q_norm_a_2, k_norm_a_2, conv_w_2, conv_b_2, conv_ln_g_2, conv_ln_b_2, w_in_cd_2,
        w_out_cd_2, q_norm_c_2, k_norm_c_2, sink_c_2, pool_w_2, pool_scale_2, rt_grp_w_2,
        rt_grp_b_2, rt_exp_w_2, rt_exp_b_2, ex_gate_2, ex_up_2, ex_down_2,
    )


_drawn_inputs = setup_inputs


def setup_inputs(seed=0):
    import zlib

    import numpy as np

    out = dict(_drawn_inputs(seed))
    spreads = {}
    factors = {'norm_mix': 4.647,
     'norm_ffn': 3.232,
     'a_q_gain': 8.0,
     'a_k_gain': 8.0,
     'b_q_gain': 8.0,
     'b_k_gain': 8.0,
     'ctx_2': 3.723,
     'mod_b_2': 2.802,
     'ln1_g_2': 8.0,
     'ln2_g_2': 5.759,
     'q_norm_a_2': 8.0,
     'k_norm_a_2': 8.0,
     'conv_b_2': 8.0,
     'conv_ln_g_2': 8.0,
     'conv_ln_b_2': 8.0,
     'q_norm_c_2': 8.0,
     'k_norm_c_2': 22.826,
     'sink_c_2': 8.0,
     'pool_scale_2': 8.0,
     'rt_grp_b_2': 8.0,
     'rt_exp_b_2': 8.0}
    for name, (base, spread) in spreads.items():
        noise = np.random.default_rng([zlib.crc32(name.encode()), seed]).standard_normal(out[name].shape)
        drawn = base * np.exp(spread * noise) if base else spread * noise
        out[name] = jnp.asarray(drawn.astype(out[name].dtype))
    for name, factor in factors.items():
        out[name] = (out[name] * factor).astype(out[name].dtype)
    return out
```

```python
from contextlib import ExitStack

import numpy as np

import concourse.bass as bass
from concourse import mybir


def Record(**fields):
    return type("Record", (), fields)


F32, I32, U32 = mybir.dt.float32, mybir.dt.int32, mybir.dt.uint32
ALU, ACT, AX = mybir.AluOpType, mybir.ActivationFunctionType, mybir.AxisListType.X

P = 128
D = 1024
KD = D // P
SEQ = CTX = 256
HD = 64
SCALE = HD ** -0.5
EPS = 1e-6
NEG = -1e30
BANK = 512
GROUPS = ((128, 1), (512, 4), (2048, 16))
NG = len(GROUPS)
GH = 8
A_HEADS, B_HEADS = NG * GH, 16
BUCKETS, MAX_DIST = 32, 2048
TOEP = 384
D_FF = 4 * D
FF_TILES = D_FF // BANK
MOD_N = 6 * D // BANK
TAPS = 31
POOLS = (2, 4, 8, 16)
WINDOW = 128
EG, EPG = 4, 8
NE = EG * EPG
CAP = 64
X_TURNED, X_OUT, GATE_UP, SWISH, HIDDEN, H_TURNED, H_OUT, Y_COPIED = range(1, 9)
STEPS = Y_COPIED
RING = 6
TILE = 4096


def blocks_most(tokens):
    return (2 * tokens + NE * (CAP - 1)) // CAP


OVER = blocks_most(SEQ + CTX) - NE
NB = NE + OVER
YROWS = NB * CAP


def bucket(dist):
    n = np.maximum(dist, 0)
    exact = BUCKETS // 2
    nf = np.maximum(n, 1).astype(np.float32)
    large = exact + (np.log(nf / np.float32(exact)) / np.float32(np.log(MAX_DIST / exact))
                     * np.float32(BUCKETS - exact)).astype(np.int32)
    return np.where(n < exact, n, np.minimum(large, BUCKETS - 1))


CONST = {}


def shape_constants():
    p = np.arange(P)
    parts = {}
    parts["ident"] = np.eye(P)
    parts["before"] = (p[:, None] < p[None, :]).astype(np.float32)
    parts["slot"] = np.tile(np.arange(CAP), (P, 1))
    parts["block"] = np.tile(np.arange(NB), (P, 1))
    parts["expert"] = np.tile(np.arange(NE), (P, 1))
    parts["group"] = np.tile(np.arange(NE) // EPG, (P, 1))
    parts["over"] = np.tile(np.repeat(np.arange(OVER), NE), (P, 1))
    parts["token"] = p[:, None] + P * np.arange(4)[None, :]
    parts["eps"] = np.full((P, 1), EPS)
    parts["quad"] = np.stack([(p % 32 == j) for j in range(2)], 1)
    col = 0
    for name, a in parts.items():
        CONST[name] = (col, col + a.shape[1])
        col += a.shape[1]
    table = np.concatenate([np.asarray(a, np.float32).reshape(P, -1) for a in parts.values()], 1)
    u = np.arange(TOEP)
    dist = SEQ - 1 - u
    onehot = ((bucket(dist)[None, :] == np.arange(BUCKETS)[:, None]) & (dist >= 0)).astype(np.float32)
    masks = []
    for window, dil in GROUPS:
        ok = (dist >= 0) & (dist <= window) & (dist % dil == 0)
        masks += [np.where(ok, 0.0, NEG)] * GH
    causal = [np.where(dist >= 0, 0.0, NEG)] * B_HEADS
    diag = np.zeros((BUCKETS, 3 * TOEP), np.float32)
    diag[:, :TOEP] = onehot
    diag[:A_HEADS, TOEP:2 * TOEP] = np.stack(masks)
    diag[:B_HEADS, 2 * TOEP:] = np.stack(causal)
    pos = np.arange(SEQ)
    inv = (np.float32(10000.0) ** (-np.arange(HD // 4, dtype=np.float32) / np.float32(HD // 4))).astype(np.float32)
    ang = np.concatenate([(pos // 64).astype(np.float32)[:, None] * inv,
                          (pos % 64).astype(np.float32)[:, None] * inv], 1).astype(np.float32)
    cos, sin = np.cos(ang), np.sin(ang)
    rope = np.stack([np.concatenate([cos, cos], 1), np.concatenate([-sin, sin], 1)])
    rope = rope.reshape(2, 2, P, HD).transpose(2, 0, 1, 3).reshape(P, -1).astype(np.float32)
    q = np.arange(P)[:, None, None] + P * np.arange(2)[None, :, None]
    k = np.arange(SEQ + CTX)[None, None, :]
    window = np.where((abs(q - k) <= WINDOW) | (k >= SEQ), 0.0, NEG).astype(np.float32)
    band = np.zeros((SEQ, len(POOLS), SEQ), np.float32)
    for g, w in enumerate(POOLS):
        lo = np.clip(pos - w // 2, 0, SEQ)
        hi = np.clip(pos - w // 2 + w, 0, SEQ)
        inside = (pos[:, None] >= lo[None, :]) & (pos[:, None] < hi[None, :])
        band[:, g, :] = inside / (hi - lo).astype(np.float32)[None, :] - np.eye(SEQ)
    band = band.reshape(2, P, len(POOLS), SEQ).transpose(1, 0, 2, 3).reshape(P, -1)
    return table, diag, rope, window, np.ascontiguousarray(band.astype(np.float32))


VEC = {}
_row = 0
for _name, _rows in (("norm_mix", 16), ("norm_ffn", 16), ("ln1_g_2", 16), ("ln2_g_2", 16), ("conv_b_2", 4),
                     ("conv_ln_g_2", 4), ("conv_ln_b_2", 4), ("pool_scale_2", 4), ("c_2", 8), ("c_ctx_2", 8),
                     ("a_q_gain", 1), ("a_k_gain", 1), ("b_q_gain", 1), ("b_k_gain", 1),
                     ("q_norm_a_2", 1), ("k_norm_a_2", 1), ("q_norm_c_2", 1), ("k_norm_c_2", 1)):
    VEC[_name] = _row
    _row += _rows
VROWS = _row
N_VLOADS = len(VEC) + 8
ARENA = 19352


class Ring:

    def __init__(self):
        self.used, self.next = [0] * RING, 0

    def tiles(self, n, trips=1):
        slots = [(self.next + i) % RING for i in range(n)]
        per = [slots.count(s) for s in range(RING)]
        out = [Record(slot=s, first=self.used[s] + slots[:i].count(s), per=per[s])
               for i, s in enumerate(slots)]
        for s in range(RING):
            self.used[s] += per[s] * trips
        self.next += n
        return out


class Count:

    def __init__(self, eng, sem, start=0):
        self.eng, self.sem, self.n = eng, sem, start

    def __call__(self, ins):
        ins.then_inc(self.sem, 1)
        self.n += 1

    def wait(self):
        self.eng.wait_ge(self.sem, self.n)


def build(nc, ins, out):
    ctx = ExitStack()
    with ctx:
        ctx.enter_context(nc.allow_non_contiguous_dma("column tiles of the weights, bias diagonals, vectors"))

        def sb(name, shape, dt=F32):
            return ctx.enter_context(nc.sbuf_tensor(name, shape, dt))

        def sem(name):
            return ctx.enter_context(nc.semaphore(name))

        def sems(stage, names):
            return Record(**{n: sem(f"{stage}_{n}") for n in names.split()})

        kinds, counts = {}, {}

        def shared(kind, **totals):
            if kind not in kinds:
                kinds[kind] = (sems(kind, " ".join(totals)), {n: 0 for n in totals})
            sem_set, base = kinds[kind]
            before = Record(**base)
            for n, total in totals.items():
                base[n] += total
            return sem_set, before

        def dram(name, shape):
            return nc.dram_tensor(name, shape, F32, kind="Internal").ap()

        ring = sb("ring", [P, RING, TILE])
        hx = sb("hx", [P, 2, D])
        xn = sb("xn", [P, 2, D])
        n_const = max(b for _, b in CONST.values())
        const = sb("const", [P, n_const])
        ones = sb("ones", [P, P])[:, :]
        vec = sb("vec", [P, VROWS])
        silu_c = sb("silu_c", [P, KD, 32])
        modp = sb("modp", [P, 2, BANK])
        modrow = sb("modrow", [2, 2, BANK])
        modbias = sb("modbias", [2, 2, BANK])
        small = sb("small", [P, 144])
        modT = sb("modT", [P, 2 * 96])
        modg = sb("modg", [P, 8 * KD])
        convw = modp[:, :, :].rearrange("p a b -> p (a b)")[:, 0:4 * TAPS].rearrange("p (c k) -> p c k", c=4)
        arena = sb("arena", [P, ARENA])
        PS = ctx.enter_context(nc.psum_tensor("PS", [P, 8, BANK], F32))

        def C(name):
            a, b = CONST[name]
            return const[:, a:b]

        ident = C("ident")

        def area(off, *shape):
            n = int(np.prod(shape))
            assert off + n <= ARENA, (off, n)
            a = arena[:, off:off + n]
            if len(shape) == 2:
                return a.rearrange("p (a b) -> p a b", a=shape[0])
            if len(shape) == 3:
                return a.rearrange("p (a b c) -> p a b c", a=shape[0], b=shape[1])
            return a

        XT = area(0, KD, SEQ + CTX)
        XL = area(0, KD, SEQ)

        def vcol(name, i=0, n=1):
            return vec[:, VEC[name] + i:VEC[name] + i + n]

        def w8(tile, n=BANK):
            return ring[:, tile.slot, 0:KD * n].rearrange("p (k n) -> p k n", k=KD)

        def w4(tile):
            return ring[:, tile.slot, :].rearrange("p (k n) -> p k n", k=4)

        bias_a = dram("bias_a", (A_HEADS, P, SEQ))
        bias_b = dram("bias_b", (B_HEADS, P, SEQ))
        tokens_d = dram("tokens_d", (SEQ + CTX, D))
        rows_d = dram("rows_d", (YROWS, D))
        mod_d = dram("mod_d", (2, 2, 6 * D))

        R = Ring()
        T_aqkv = R.tiles(9)
        T_awo = R.tiles(1)
        T_ffn = [None, None]
        T_bqkv = T_bwo = None
        for l in range(2):
            head = R.tiles(3)
            body = R.tiles(8, trips=3)
            tail = R.tiles(1)
            T_ffn[l] = Record(head=head, body=body, tail=tail)
            if l == 0:
                T_bqkv = R.tiles(6)
                T_bwo = R.tiles(2)
        T_ab, T_abo = R.tiles(4), R.tiles(2)
        T_moe = [R.tiles(6, trips=NE // 2), None]
        T_cd, T_cdo = R.tiles(3), R.tiles(2)
        T_moe[1] = R.tiles(6, trips=NE // 2)

        full = [sem(f"tile_full{s}") for s in range(RING)]
        used = [sem(f"tile_used{s}") for s in range(RING)]

        def use(tile, i=0):
            return i * tile.per + tile.first

        def tile_full(eng, tile, i=0):
            eng.wait_ge(full[tile.slot], (use(tile, i) + 1) * 16)

        def tile_used(eng, tile, i=0):
            eng.wait_ge(used[tile.slot], use(tile, i) + 1)

        s_const, s_x = sem("const_loaded"), sem("x_loaded")
        s_set = sem("silu_zeroed_ones_set")
        s_vrows, s_vT, s_vec, s_silu = sem("vec_rows_loaded"), sem("vec_transposed"), sem("vec_ready"), sem("silu_ready")
        s_diag, s_brow, s_bsb, s_bd = sem("diag_loaded"), sem("bias_rows"), sem("bias_rows_ready"), sem("bias_stored")

        def norm_stage(src, dst, gain, shift, ready):
            s, b = shared("norm", squares=2, root=2, inverse=2, norm=2, turned=4, out=8)
            return Record(src=src, dst=dst, gain=gain, shift=shift, ready=ready, s=s, b=b,
                           turned=(s.turned, b.turned + 4), done=[(s.out, b.out + 8)],
                           read=[(s.norm, b.norm + 2), (s.squares, b.squares + 2)])

        def at(eng, *events):
            for s, v in events:
                eng.wait_ge(s, v)


        def pe_norm(pe, n):
            for t in range(2):
                pe.wait_ge(n.s.norm, n.b.norm + t + 1)
                for k in range(KD):
                    col = (k % 2) * SEQ + t * P
                    mm = pe.transpose(PS[:, k // 2, col:col + P], xn[:, t, k * P:(k + 1) * P], ident)
                    if t == 1 and k % 2:
                        mm.then_inc(n.s.turned, 1)

        def root(act, dst, total, n):
            return act.activation(dst, total, ACT.Sqrt, bias=C("eps"), scale=1.0 / n)

        def act_norm(act, n, table_ready=()):
            for s, v in n.ready:
                act.wait_ge(s, v)
            for t in range(2):
                act.activation(xn[:, t], n.src[:, t], ACT.Square, accum_out=small[:, t:t + 1])\
                   .then_inc(n.s.squares, 1)
                act.wait_ge(n.s.squares, n.b.squares + t + 1)
                root(act, small[:, 4 + t:5 + t], small[:, t:t + 1], D).then_inc(n.s.root, 1)
            at(act, *table_ready)
            norm_out(act, n, 0)

        def dve_norm(dve, n, between=None):
            at(dve, *n.ready)
            for t in range(2):
                dve.wait_ge(n.s.root, n.b.root + t + 1)
                dve.reciprocal(small[:, 6 + t:7 + t], small[:, 4 + t:5 + t]).then_inc(n.s.inverse, 1)
                dve.wait_ge(n.s.inverse, n.b.inverse + t + 1)
                dve.tensor_scalar(xn[:, t], n.src[:, t], small[:, 6 + t:7 + t], None, ALU.mult)\
                   .then_inc(n.s.norm, 1)
            if between:
                between()
            norm_out(dve, n, 1)

        def norm_out(eng, n, half):
            for k in range(4 * half, 4 * half + 4):
                if k % 2 == 0:
                    eng.wait_ge(n.s.turned, n.b.turned + k // 2 + 1)
                src, dst = PS[:, k // 2, (k % 2) * SEQ:(k % 2 + 1) * SEQ], n.dst[:, k, :]
                g, b = n.gain[:, k:k + 1], None if n.shift is None else n.shift[:, k:k + 1]
                if half == 0:
                    if b is None:
                        eng.activation(dst, src, ACT.Copy, scale=g).then_inc(n.s.out, 1)
                    else:
                        eng.activation(dst, src, ACT.Identity, scale=g, bias=b).then_inc(n.s.out, 1)
                elif b is None:
                    eng.tensor_scalar(dst, src, g, None, ALU.mult).then_inc(n.s.out, 1)
                else:
                    eng.tensor_scalar(dst, src, g, b, ALU.mult, ALU.add).then_inc(n.s.out, 1)


        def qkv_stage(src, units, normed, squares, rotated=None):
            n = sum(bool(w.qk) for w in units)
            s, b = shared("heads", product=len(units) - len({id(w.tile) for w in units}), square=n, sum=n, 
                          root=n, inverse=n, norm=n, turned=n, out=n, value=sum(w.v is not None for w in units),
                          rotate=0)
            q = Record(src=src, units=units, normed=normed, squares=squares, rotated=rotated,
                        s=s, b=b)
            products = n_qk = n_v = 0
            for u, unit in enumerate(units):
                unit.first = u == 0 or units[u - 1].tile is not unit.tile
                unit.last = u == len(units) - 1 or units[u + 1].tile is not unit.tile
                if unit.last:
                    unit.done = (used[unit.tile.slot], unit.tile.first + 1)
                else:
                    products += 1
                    unit.done = (s.product, b.product + products)
                unit.free = []
                if unit.qk:
                    unit.n, n_qk = n_qk, n_qk + 1
                    unit.free.append((s.norm, b.norm + n_qk))
                if unit.v is not None:
                    n_v += 1
                    unit.free.append((s.value, b.value + n_v))
            q.qks = [u for u in units if u.qk]
            q.done = [(s.out, b.out + n_qk), (s.value, b.value + n_v)]
            return q

        def unit(tile, t, width=BANK, qk=None, v=None, v_src=0):
            return Record(tile=tile, t=t, width=width, qk=qk, v=v, v_src=v_src)

        def heads(n, dst, gain=None, rope=None, dup=1):
            return Record(n=n, dst=dst, gain=gain, rope=rope, dup=dup, pairs=n * dup // 2)

        def pe_qkv(pe, q):
            waiting = None
            for u, w in enumerate(q.units):
                if w.first:
                    tile_full(pe, w.tile)
                if u >= 4:
                    at(pe, *q.units[u - 4].free)
                for k in range(KD):
                    mm = pe.matmul(PS[:, u % 4, 0:w.width], q.src[:, k, w.t * P:(w.t + 1) * P],
                                   w8(w.tile, w.width)[:, k, :], start=(k == 0), stop=(k == KD - 1))
                mm.then_inc(w.done[0], 1)
                if waiting:
                    pe_turn_heads(pe, q, waiting)
                waiting = w if w.qk else None
            if waiting:
                pe_turn_heads(pe, q, waiting)

        def pe_turn_heads(pe, q, w):
            pe.wait_ge(q.s.norm, q.b.norm + w.n + 1)
            if w.n >= 4:
                pe.wait_ge(q.s.out, q.b.out + w.n - 3)
            for j in range(w.qk.pairs):
                mm = pe.transpose(PS[:, 4 + w.n % 4, j * P:(j + 1) * P], q.normed[:, w.n % 3, j * P:(j + 1) * P],
                                  ident)
            mm.then_inc(q.s.turned, 1)

        def act_qkv(act, q):
            waiting = []
            for u, w in enumerate(q.units):
                at(act, w.done)
                if w.v is not None:
                    n = w.width - w.v_src
                    act.copy(w.v, PS[:, u % 4, w.v_src:w.v_src + n]).then_inc(q.s.value, 1)
                if w.qk:
                    n = w.qk.n * HD
                    if w.n >= 2:
                        act.wait_ge(q.s.sum, q.b.sum + w.n - 1)
                    act.activation(q.squares[:, w.n % 2, 0:n], PS[:, u % 4, 0:n], ACT.Square)\
                       .then_inc(q.s.square, 1)
                    act.wait_ge(q.s.sum, q.b.sum + w.n + 1)
                    root(act, stat(2, w.n)[:, 0:w.qk.n], stat(0, w.n)[:, 0:w.qk.n], HD).then_inc(q.s.root, 1)
                if waiting:
                    act_heads_out(act, q, waiting.pop())
                if w.qk:
                    waiting.append(w)
            if waiting:
                act_heads_out(act, q, waiting.pop())

        def act_heads_out(act, q, w):
            act.wait_ge(q.s.turned, q.b.turned + w.n + 1)
            src = PS[:, 4 + w.n % 4, 0:w.qk.pairs * P].rearrange("p (a b) -> p a b", a=w.qk.pairs)
            if w.qk.gain is None:
                act.copy(w.qk.dst, src).then_inc(q.s.out, 1)
            else:
                act.activation(w.qk.dst, src, ACT.Copy, scale=w.qk.gain).then_inc(q.s.out, 1)

        def stat(i, n):
            return small[:, 16 + (i * 2 + n % 2) * 8:24 + (i * 2 + n % 2) * 8]

        def dve_qkv(dve, q):
            rotate = counts.setdefault("rotate", Count(dve, q.s.rotate))
            for u, w in enumerate(q.units):
                if not w.qk:
                    continue
                h = w.qk.n
                dve.wait_ge(q.s.square, q.b.square + w.n + 1)
                dve.tensor_reduce(stat(0, w.n)[:, 0:h],
                                  q.squares[:, w.n % 2, 0:h * HD].rearrange("p (h d) -> p h d", h=h),
                                  AX, ALU.add).then_inc(q.s.sum, 1)
                dve.wait_ge(q.s.root, q.b.root + w.n + 1)
                dve.reciprocal(stat(3, w.n)[:, 0:h], stat(2, w.n)[:, 0:h]).then_inc(q.s.inverse, 1)
                dve.wait_ge(q.s.inverse, q.b.inverse + w.n + 1)
                if w.n >= 3:
                    dve.wait_ge(q.s.turned, q.b.turned + w.n - 2)
                at(dve, w.done)
                src = PS[:, u % 4, 0:h * HD].rearrange("p (h d) -> p h d", h=h)
                inv = stat(3, w.n)[:, 0:h].unsqueeze(2).to_broadcast([P, h, HD])
                dst = q.normed[:, w.n % 3, 0:h * w.qk.dup * HD].rearrange("p (h c d) -> p h c d", c=w.qk.dup, d=HD)
                if w.qk.rope is None:
                    for c in range(w.qk.dup):
                        ins = dve.tensor_tensor(dst[:, :, c, :], src, inv, ALU.mult)
                    ins.then_inc(q.s.norm, 1)
                    continue
                straight, crossed = w.qk.rope
                r = [q.rotated[:, i, 0:h * HD].rearrange("p (h d) -> p h d", h=h) for i in range(3)]
                half = HD // 2
                rotate(dve.tensor_tensor(r[0], src, inv, ALU.mult))
                rotate.wait()
                rotate(dve.tensor_tensor(r[1], r[0], straight.unsqueeze(1).to_broadcast([P, h, HD]), ALU.mult))
                for a, b in ((0, half), (half, 0)):
                    rotate(dve.tensor_tensor(r[2][:, :, a:a + half], r[0][:, :, b:b + half],
                                             crossed[:, a:a + half].unsqueeze(1).to_broadcast([P, h, half]),
                                             ALU.mult))
                rotate.wait()
                for c in range(w.qk.dup):
                    ins = dve.tensor_tensor(dst[:, :, c, :], r[1], r[2], ALU.add)
                ins.then_inc(q.s.norm, 1)


        def attention(steps, ready, biased, bufs):
            n, n_sink = len(steps), sum(st.sink is not None for st in steps)
            s, b = shared("softmax", scores=n, biased=n * biased, top=n, top2=n_sink, negated=n, exps=n, sink=n_sink,
                          turned=n, copied=n, values=n, inverse=n, total=n_sink, out=n)
            a = Record(steps=steps, ready=ready, s=s, b=b, biased=biased, **bufs)
            a.read, a.read0 = (s.biased, b.biased) if biased else (s.exps, b.exps)
            a.done = [(s.out, b.out + n)]
            return a

        def pe_attention(pe, a):
            at(pe, *a.ready)
            for i in range(len(a.steps) + 3):
                if i < len(a.steps):
                    if i >= 2:
                        pe.wait_ge(a.read, a.read0 + i - 1)
                    for col, lhs, rhs in a.steps[i].scores:
                        n = rhs.shape[-1]
                        bank, c = 2 * (i % 2) + col // BANK, col % BANK
                        mm = pe.matmul(PS[:, bank, c:c + n], lhs, rhs, start=True, stop=True)
                    mm.then_inc(a.s.scores, 1)
                j = i - 2
                if 0 <= j < len(a.steps):
                    pe.wait_ge(a.s.exps, a.b.exps + j + 1)
                    if j >= 1:
                        pe.wait_ge(a.s.copied, a.b.copied + j)
                    for b in range(a.steps[j].width // P):
                        mm = pe.transpose(PS[:, 4 + b // 4, (b % 4) * P:(b % 4 + 1) * P],
                                          a.probs[:, j % 2, b * P:(b + 1) * P], ident)
                    mm.then_inc(a.s.turned, 1)
                j = i - 3
                if 0 <= j < len(a.steps):
                    pe.wait_ge(a.s.copied, a.b.copied + j + 1)
                    if j >= 2:
                        pe.wait_ge(a.s.out, a.b.out + j - 1)
                    vs = a.steps[j].values
                    for b, v in enumerate(vs):
                        mm = pe.matmul(PS[:, 6 + j % 2, 0:HD], a.probsT[:, j % 2, b * P:(b + 1) * P], v,
                                       start=(b == 0), stop=(b == len(vs) - 1))
                    mm.then_inc(a.s.values, 1)

        def top_col(j, i):
            return small[:, 96 + i * 4 + j % 4:97 + i * 4 + j % 4]

        def act_attention(act, a, between=None):
            for i in range(len(a.steps) + 2):
                j = i - 2
                if j >= 0:
                    act.wait_ge(a.s.turned, a.b.turned + j + 1)
                    if j >= 2:
                        act.wait_ge(a.s.values, a.b.values + j - 1)
                    act.copy(a.probsT[:, j % 2, 0:a.steps[j].width],
                             PS[:, 4:6, :].rearrange("p a b -> p (a b)")[:, 0:a.steps[j].width])\
                       .then_inc(a.s.copied, 1)
                if i < len(a.steps):
                    st = a.steps[i]
                    act.wait_ge(a.s.negated, a.b.negated + i + 1)
                    if i >= 2:
                        act.wait_ge(a.s.turned, a.b.turned + i - 1)
                    if st.sink is not None:
                        act.activation(top_col(i, 4), st.sink, ACT.Exp, bias=top_col(i, 1)).then_inc(a.s.sink, 1)
                    if a.biased:
                        src, scale = a.logits[:, i % 2, 0:st.width], 1.0
                    else:
                        src, scale = PS[:, 2 * (i % 2), 0:st.width], SCALE
                    act.activation(a.probs[:, i % 2, 0:st.width], src, ACT.Exp, bias=top_col(i, 1), scale=scale,
                                   accum_out=top_col(i, 2)).then_inc(a.s.exps, 1)
                if between:
                    between(i)

        def dve_attention(dve, a, between=None):
            n_sink = 0
            for i in range(len(a.steps) + 3):
                if i < len(a.steps):
                    st = a.steps[i]
                    dve.wait_ge(a.s.scores, a.b.scores + i + 1)
                    scores = PS[:, 2 * (i % 2):2 * (i % 2) + 2, :].rearrange("p a b -> p (a b)")[:, 0:st.width]
                    if a.biased:
                        if st.bias_ready:
                            at(dve, *st.bias_ready)
                        if i >= 2:
                            dve.wait_ge(a.s.exps, a.b.exps + i - 1)
                        dst = a.logits[:, i % 2, 0:st.width]
                        g = st.bias.shape[1] if len(st.bias.shape) == 3 else 1
                        if g > 1:
                            scores = scores.rearrange("p (g k) -> p g k", g=g)
                            ins = dve.scalar_tensor_tensor(dst.rearrange("p (g k) -> p g k", g=g), scores, SCALE,
                                                           st.bias, ALU.mult, ALU.add)
                        else:
                            ins = dve.scalar_tensor_tensor(dst, scores, SCALE, st.bias, ALU.mult, ALU.add)
                        ins.then_inc(a.s.biased, 1)
                        dve.wait_ge(a.s.biased, a.b.biased + i + 1)
                        src, scale = dst, -1.0
                    else:
                        src, scale = scores, -SCALE
                    dve.tensor_reduce(top_col(i, 0), src, AX, ALU.max).then_inc(a.s.top, 1)
                    dve.wait_ge(a.s.top, a.b.top + i + 1)
                    if st.sink is not None:
                        dve.tensor_scalar(top_col(i, 5), top_col(i, 0), st.sink, None, ALU.max)\
                           .then_inc(a.s.top2, 1)
                        n_sink += 1
                        dve.wait_ge(a.s.top2, a.b.top2 + n_sink)
                    dve.tensor_scalar(top_col(i, 1), top_col(i, 5 if st.sink is not None else 0), scale, None,
                                      ALU.mult).then_inc(a.s.negated, 1)
                if between:
                    between(i)
                j = i - 3
                if j >= 0:
                    dve.wait_ge(a.s.exps, a.b.exps + j + 1)
                    total = top_col(j, 2)
                    if a.steps[j].sink is not None:
                        dve.wait_ge(a.s.sink, a.b.sink + j + 1)
                        dve.tensor_tensor(top_col(j, 6), total, top_col(j, 4), ALU.add).then_inc(a.s.total, 1)
                        dve.wait_ge(a.s.total, a.b.total + j + 1)
                        total = top_col(j, 6)
                    dve.reciprocal(top_col(j, 3), total).then_inc(a.s.inverse, 1)
                    dve.wait_ge(a.s.inverse, a.b.inverse + j + 1)
                    dve.wait_ge(a.s.values, a.b.values + j + 1)
                    dve.tensor_scalar(a.steps[j].out, PS[:, 6 + j % 2, 0:HD], top_col(j, 3), None, ALU.mult)\
                       .then_inc(a.s.out, 1)


        def turn_stage(src, dst, tiles, width, ready):
            parts = [(t, c) for t in range(tiles) for c in range(width // BANK)]
            s, b = shared("turn", turned=len(parts), out=len(parts))
            return Record(src=src, dst=dst, parts=parts, ready=ready, s=s, b=b,
                           done=[(s.out, b.out + len(parts))])

        def pe_turn(pe, x):
            at(pe, *x.ready)
            for n, (t, c) in enumerate(x.parts):
                if n >= 4:
                    pe.wait_ge(x.s.out, x.b.out + n - 3)
                for k in range(4):
                    col = c * BANK + k * P
                    mm = pe.transpose(PS[:, n % 4, k * P:(k + 1) * P], x.src[:, t, col:col + P], ident)
                mm.then_inc(x.s.turned, 1)

        def act_turn(act, x):
            for n, (t, c) in enumerate(x.parts):
                act.wait_ge(x.s.turned, x.b.turned + n + 1)
                act.copy(x.dst[:, 4 * c:4 * c + 4, t * P:(t + 1) * P],
                         PS[:, n % 4, :].rearrange("p (a b) -> p a b", a=4)).then_inc(x.s.out, 1)


        def proj_stage(src, units, ready):
            n = len(units)
            s, b = shared("project", product=n - len({id(w.tile) for w in units}),
                          gated=n * (units[0].gate is not None), added=n)
            products = 0
            for u, w in enumerate(units):
                if u == len(units) - 1 or units[u + 1].tile is not w.tile:
                    w.done = (used[w.tile.slot], w.tile.first + 1)
                else:
                    products += 1
                    w.done = (s.product, b.product + products)
            return Record(src=src, units=units, s=s, b=b, ready=ready, done=[(s.added, b.added + n)])

        def pe_proj(pe, x):
            at(pe, *x.ready)
            for u, w in enumerate(x.units):
                tile_full(pe, w.tile)
                if u >= 8:
                    pe.wait_ge(x.s.added, x.b.added + u - 7)
                for i, (k, rhs) in enumerate(w.terms):
                    mm = pe.matmul(PS[:, u % 8, :], x.src[:, k, w.t * P:(w.t + 1) * P], rhs,
                                   start=(i == 0), stop=(i == len(w.terms) - 1))
                mm.then_inc(w.done[0], 1)

        def dve_proj(dve, x):
            for u, w in enumerate(x.units):
                at(dve, w.done)
                src = PS[:, u % 8, :]
                if w.gate is not None:
                    dve.tensor_tensor(gated(u), src, w.gate, ALU.mult).then_inc(x.s.gated, 1)
                    dve.wait_ge(x.s.gated, x.b.gated + u + 1)
                    src = gated(u)
                dve.tensor_tensor(w.res, w.res, src, ALU.add).then_inc(x.s.added, 1)

        def gated(u):
            return xn[:, u % 2, 0:BANK]


        def ffn_stage(l, tiles, ready):
            two = 2 * FF_TILES
            s, b = shared("mlp", w1=FF_TILES, relu=two, hidden=two, turned=two, out=two, added=4, mod_copied=MOD_N,
                          mod_sum=MOD_N, mod_row=MOD_N, mod_bias0=8 * MOD_N, mod_bias1=8 * MOD_N,
                          mod_out0=8 * MOD_N, mod_out1=8 * MOD_N)
            return Record(l=l, t=tiles, ready=ready, s=s, b=b, done=[(s.added, b.added + 4)],
                           mod_stored=[(s.mod_out0, b.mod_out0 + 8 * MOD_N),
                                       (s.mod_out1, b.mod_out1 + 8 * MOD_N)])

        hidden = area(2048, 2, BANK)
        hiddenT = area(3072, 4, 2 * P)
        relu = area(4096, 2, BANK)

        def pe_ffn(pe, f):
            s, b0 = f.s, f.b

            def w1(tile, j, i=0):
                tile_full(pe, tile, i)
                if not isinstance(j, int) or j:
                    pe.wait_ge(s.relu, b0.relu + 2 * j)
                for t in range(2):
                    for k in range(KD):
                        mm = pe.matmul(PS[:, t, :], XL[:, k, t * P:(t + 1) * P], w8(tile)[:, k, :],
                                       start=(k == 0), stop=(k == KD - 1))
                    mm.then_inc(used[tile.slot] if t else s.w1, 1)

            def turn(j, mods=False):
                for t in range(2):
                    pe.wait_ge(s_const, 16)
                    pe.wait_ge(s.hidden, b0.hidden + 2 * j + t + 1)
                    if mods:
                        pe.wait_ge(s.mod_row, b0.mod_row + 2 * j - 3 + t)
                    for k in range(4):
                        mm = pe.transpose(PS[:, 2 + t, k * P:(k + 1) * P],
                                          hidden[:, t, :].rearrange("p (m k) -> p k m", k=4)[:, k, :], ident)
                    mm.then_inc(s.turned, 1)

            def w2(tile, j, i=0, first=False, last=False, between=None):
                tile_full(pe, tile, i)
                pe.wait_ge(s.out, b0.out + 2 * (j + 1))
                for t in range(2):
                    for h in range(2):
                        for k in range(4):
                            mm = pe.matmul(PS[:, 4 + 2 * t + h, :], hiddenT[:, k, t * P:(t + 1) * P],
                                           w4(tile)[:, k, h * BANK:(h + 1) * BANK],
                                           start=first and k == 0, stop=last and k == 3)
                    if t == 0 and between:
                        between()
                mm.then_inc(used[tile.slot], 1)

            def mod_part(tile, n, i, b, j):
                tile_full(pe, tile, i)
                pe.wait_ge(s.out, b0.out + 2 * j)
                for h in range(2):
                    for g in range(4):
                        k = 4 * h + g
                        mm = pe.matmul(PS[32 * g:32 * g + 32, 2 + b, :], silu_c[:, k, :], w8(tile)[:, k, :],
                                       start=(h == 0), stop=(h == 1))
                mm.then_inc(used[tile.slot], 1)

            def mod_sum(n, b):
                pe.wait_ge(s.mod_copied, b0.mod_copied + n + 1)
                pe.matmul(PS[0:2, 2 + b, :], C("quad"), modp[:, b, :], start=True, stop=True)\
                  .then_inc(s.mod_sum, 1)

            T = f.t
            at(pe, *f.ready)
            w1(T.head[0], 0)
            turn(0)
            w1(T.head[1], 1)
            w2(T.head[2], 0, first=True)
            turn(1)
            with pe.Fori(0, 3) as i:
                for h in range(2):
                    j = 2 * i + 2 + h
                    m = 4 * i + 2 * h
                    w1(T.body[4 * h], j, i)
                    mod_part(T.body[4 * h + 1], m, i, 0, j)
                    mod_part(T.body[4 * h + 2], m + 1, i, 1, j)

                    def sums(m=m):
                        mod_sum(m, 0)
                        mod_sum(m + 1, 1)
                    w2(T.body[4 * h + 3], j - 1, i, between=sums)
                    turn(j, mods=True)
            w2(T.tail[0], FF_TILES - 1, last=True)

        def ffn_passes(eng, f, step, mods):
            step(0, f.t.head[0], 0)
            step(1, f.t.head[1], 0)
            with eng.Fori(0, 3) as i:
                for h in range(2):
                    def between(h=h):
                        mods(2 * i + h, [f.t.body[4 * h + 1], f.t.body[4 * h + 2]], i)
                    step(2 * i + 2 + h, f.t.body[4 * h], i, between)

        def act_ffn(act, f):
            s, b0 = f.s, f.b

            def step(j, tile, i, mid=None):
                for t in range(2):
                    if t:
                        tile_used(act, tile, i)
                    else:
                        act.wait_ge(s.w1, b0.w1 + j + 1)
                    act.activation(relu[:, t, :], PS[:, t, :], ACT.Relu).then_inc(s.relu, 1)
                if mid:
                    mid()
                act.wait_ge(s.turned, b0.turned + 2 * j + 1)
                act.copy(hiddenT[:, :, 0:P], PS[:, 2, :].rearrange("p (a b) -> p a b", a=4)).then_inc(s.out, 1)

            def mods(r, tiles, i):
                for b in range(2):
                    tile_used(act, tiles[b], i)
                    act.copy(modp[:, b, :], PS[:, 2 + b, :]).then_inc(s.mod_copied, 1)

            ffn_passes(act, f, step, mods)

        def dve_ffn(dve, f):
            s, b0 = f.s, f.b

            def step(j, tile, i, mid=None):
                for t in range(2):
                    dve.wait_ge(s.relu, b0.relu + 2 * j + t + 1)
                    dve.tensor_tensor(hidden[:, t, :], relu[:, t, :], relu[:, t, :], ALU.mult)\
                       .then_inc(s.hidden, 1)
                if mid:
                    mid()
                dve.wait_ge(s.turned, b0.turned + 2 * j + 2)
                dve.tensor_copy(hiddenT[:, :, P:2 * P], PS[:, 3, :].rearrange("p (a b) -> p a b", a=4))\
                   .then_inc(s.out, 1)

            def mods(r, tiles, i):
                for b in range(2):
                    dve.wait_ge(s.mod_sum, b0.mod_sum + 2 * r + b + 1)
                    dve.wait_ge((s.mod_bias0, s.mod_bias1)[b], (r + 1) * 16 + b0.mod_bias0)
                    dve.tensor_tensor(modrow[:, b, :], PS[0:2, 2 + b, :], modbias[:, b, :], ALU.add)\
                       .then_inc(s.mod_row, 1)

            ffn_passes(dve, f, step, mods)
            tile_used(dve, f.t.tail[0])
            for t in range(2):
                for h in range(2):
                    r = hx[:, t, h * BANK:(h + 1) * BANK]
                    dve.tensor_tensor(r, r, PS[:, 4 + 2 * t + h, :], ALU.add).then_inc(s.added, 1)

        def pool_ffn(pool, f):
            s, b0 = f.s, f.b
            biases, outs = (s.mod_bias0, s.mod_bias1), (s.mod_out0, s.mod_out1)

            def load(r, b):
                cols = bass.ds((2 * r + b) * BANK, BANK) if not isinstance(r, int) else slice((2 * r + b) * BANK, (2 * r + b + 1) * BANK)
                pool.dma_start(modbias[:, b, :], ins["mod_b_2"][f.l:f.l + 1, cols].to_broadcast([2, BANK]))\
                    .then_inc(biases[b], 16)

            def store(r, b):
                pool.wait_ge(s.mod_row, b0.mod_row + 2 * r + b + 1)
                cols = bass.ds((2 * r + b) * BANK, BANK) if not isinstance(r, int) else slice((2 * r + b) * BANK, (2 * r + b + 1) * BANK)
                pool.dma_start(mod_d[f.l, :, cols], modrow[:, b, :]).then_inc(outs[b], 16)

            for b in range(2):
                load(0, b)
            with pool.Fori(0, MOD_N // 2 - 1) as r:
                for b in range(2):
                    store(r, b)
                    pool.wait_ge(outs[b], (r + 1) * 16 + b0.mod_out0)
                    load(r + 1, b)
            for b in range(2):
                store(MOD_N // 2 - 1, b)

        QK0, W0 = 2048, 12288
        qkT = area(QK0, 24, SEQ)
        attn_bufs = dict(logits=area(W0, 2, 768), probs=area(W0 + 1536, 2, 768), probsT=area(W0 + 3072, 2, 768))
        biasbuf = area(W0 + 4608, 2, 3, SEQ)
        qkv_bufs = dict(normed=area(W0, 3, BANK), squares=area(W0 + 1536, 2, BANK))
        s_bias = [sem("bias_full0"), sem("bias_full1")]

        n_a1 = norm_stage(hx, XL, vcol("norm_mix", 0, 8), None, [(s_x, 16)])
        v_a = area(8192, 2, A_HEADS * HD)
        units = []
        for n in range(9):
            for t in range(2):
                dst = qkT[:, 4 * n:4 * n + 4, t * P:(t + 1) * P] if n < 6 else None
                units.append(unit(T_aqkv[n], t, qk=heads(8, dst, vcol("a_q_gain" if n < 3 else "a_k_gain")) if n < 6
                                  else None, v=v_a[:, t, (n - 6) * BANK:(n - 5) * BANK] if n >= 6 else None))
        q_a = qkv_stage(XL, units, **qkv_bufs)

        def causal_steps(n_heads, groups, q_pair0, k_pair0, v, o, per_tile, bias_base):
            steps = []
            for h in range(n_heads):
                for t in range(2):
                    scores, values = [], []
                    keys = P * (t + 1)
                    for g in range(groups):
                        hh = g * GH + h if groups > 1 else h
                        pq, pk, half = q_pair0 + hh // 2, k_pair0 + hh // 2, slice((hh % 2) * HD, (hh % 2) * HD + HD)
                        scores.append((g * keys, qkT[half, pq, t * P:(t + 1) * P], qkT[half, pk, 0:keys]))
                        values += [v[:, kt, hh * HD:(hh + 1) * HD] for kt in range(t + 1)]
                    tile = h // per_tile
                    if groups > 1:
                        bias = biasbuf[:, tile % 2, :, SEQ - keys:SEQ]
                    else:
                        bias = biasbuf[:, tile % 2, h % per_tile, SEQ - keys:SEQ]
                    ready = [(s_bias[tile % 2], 16 * (bias_base + tile // 2 + 1))] if t == 0 and h % per_tile == 0 else None
                    steps.append(Record(scores=scores, values=values, width=groups * keys, bias=bias,
                                         bias_ready=ready, sink=None, out=o[:, t, h * HD:(h + 1) * HD]))
            return steps

        o_a = area(11264, 2, GH * HD)
        at_a = attention(causal_steps(GH, NG, 0, 12, v_a, o_a, 1, 0), q_a.done, True, attn_bufs)
        ot_a = area(QK0, 4, SEQ)
        tn_a = turn_stage(o_a, ot_a, 2, BANK, at_a.done)
        pr_a = proj_stage(ot_a, [
            Record(tile=T_awo[0], t=t, terms=[(k, w4(T_awo[0])[:, k, h * BANK:(h + 1) * BANK]) for k in range(4)],
                    res=hx[:, t, h * BANK:(h + 1) * BANK], gate=None) for t in range(2) for h in range(2)],
            tn_a.done)
        n_a2 = norm_stage(hx, XL, vcol("norm_ffn", 0, 8), None, pr_a.done)
        f_a = ffn_stage(0, T_ffn[0], n_a2.done)

        n_b1 = norm_stage(hx, XL, vcol("norm_mix", 8, 8), None, f_a.done)
        v_b = area(6144, 2, D)
        units = []
        for n in range(6):
            for t in range(2):
                dst = qkT[:, 4 * n:4 * n + 4, t * P:(t + 1) * P] if n < 4 else None
                units.append(unit(T_bqkv[n], t, qk=heads(8, dst, vcol("b_q_gain" if n < 2 else "b_k_gain")) if n < 4
                                  else None, v=v_b[:, t, (n - 4) * BANK:(n - 3) * BANK] if n >= 4 else None))
        q_b = qkv_stage(XL, units, **qkv_bufs)
        o_b = area(8192, 2, D)
        s_zero, s_zeroed = sem("zeros_set"), sem("rows_zeroed")
        zeros = area(8192, D)
        at_b = attention(causal_steps(B_HEADS, 1, 0, 8, v_b, o_b, 2, GH // 2),
                         q_b.done + [(s_zeroed, 16 * -(-OVER * CAP // P))], True, attn_bufs)
        ot_b = area(QK0, 8, SEQ)
        tn_b = turn_stage(o_b, ot_b, 2, D, at_b.done)
        pr_b = proj_stage(ot_b, [
            Record(tile=T_bwo[h], t=t, terms=[(k, w8(T_bwo[h])[:, k, :]) for k in range(8)],
                    res=hx[:, t, h * BANK:(h + 1) * BANK], gate=None) for h in range(2) for t in range(2)],
            tn_b.done)
        n_b2 = norm_stage(hx, XL, vcol("norm_ffn", 8, 8), None, pr_b.done)
        f_b = ffn_stage(1, T_ffn[1], n_b2.done)

        def pe_moe(pe, m):
            s, b0, T = m.s, m.b, m.tiles
            pe.wait_ge(s.weights, b0.weights + 64)
            for t in range(T):
                for k in range(KD):
                    mm = pe.matmul(PS[:, 4, t * (EG + NE):(t + 1) * (EG + NE)], XT[:, k, t * P:(t + 1) * P],
                                   m.rw[:, k, :], start=(k == 0), stop=(k == KD - 1))
            mm.then_inc(s.logits, 1)
            for t in range(T):
                if t >= 2:
                    pe.wait_ge(s.token_copied, b0.token_copied + t - 1)
                for k in range(KD):
                    mm = pe.transpose(PS[:, 2 * (t % 2) + k // 4, (k % 4) * P:(k % 4 + 1) * P],
                                      XT[:, k, t * P:(t + 1) * P], ident)
                mm.then_inc(s.token_turned, 1)
            pe.wait_ge(s.picked, b0.picked + 1)
            pe.matmul(PS[:, 5, 0:(T + 1) * NE], ones, m.prefix.rearrange("p t e -> p (t e)"), start=True, stop=False)
            mm = pe.matmul(PS[:, 5, 0:T * NE], C("before"), m.picked.rearrange("p t e -> p (t e)"),
                           start=False, stop=True)
            mm.then_inc(s.rank, 1)
            pe.wait_ge(s.placed, b0.placed + 2)
            for n in range(2 * T):
                mm = pe.matmul(PS[0:CAP, 7, 0:NB], m.slot_hot[:, n, :], m.blk_hot[:, n, :],
                               start=(n == 0), stop=(n == 2 * T - 1))
            mm.then_inc(s.ids, 1)
            pe.wait_ge(s.routed, b0.routed + 3)
            at(pe, (s.token_copied, T))
            extra = pe.value_load(m.regs[0:1, OVER:OVER + 1], min_val=0, max_val=m.over)

            def turn_x(u, done):
                for k in range(KD):
                    mm = pe.matmul(PS[:, 4 + u, k * CAP:(k + 1) * CAP],
                                   Xg[0:CAP, u, :].rearrange("p (m k) -> p k m", k=KD)[:, k, :],
                                   ident[0:CAP, 0:CAP], start=True, stop=True, is_transpose=k > 0)
                mm.then_inc(done, 1)

            def gate_up(u, gate, up, gate_done, up_done):
                xT = XgT[:, u, :].rearrange("p (k c) -> p k c", k=KD)
                for k in range(KD):
                    g = pe.matmul(PS[0:CAP, u, :], xT[:, k, :], w8(gate)[:, k, :], start=(k == 0), stop=(k == KD - 1))
                    if k == KD - 1:
                        g.then_inc(gate_done, 1) if gate_done is not None else None
                    h = pe.matmul(PS[CAP:P, u, :], xT[:, k, :], w8(up)[:, k, :], start=(k == 0), stop=(k == KD - 1))
                h.then_inc(up_done, 1)

            def turn_h(done):
                for k in range(4):
                    mm = pe.matmul(PS[:, 6, k * CAP:(k + 1) * CAP],
                                   hid[CAP:P, :].rearrange("p (m k) -> p k m", k=4)[:, k, :], ident[CAP:P, CAP:P],
                                   start=True, stop=True, is_transpose=k > 0)
                mm.then_inc(done, 1)

            def down(u, tile, done):
                for k in range(4):
                    for h in range(2):
                        mm = pe.matmul(PS[h * CAP:(h + 1) * CAP, 2 + u, :], hidT[:, k, :],
                                       w4(tile)[:, k, h * BANK:(h + 1) * BANK], start=(k == 0), stop=(k == 3))
                mm.then_inc(done, 1)

            def tokens_in(u, i):
                pe.wait_ge(s.gathered[u], b0.gathered0 + (i + 1) * 16)
                turn_x(u, s.x_turned)

            def inner(e, u, i):
                gate, up = m.T[3 * u:3 * u + 2]
                pe.wait_ge(s.xT, b0.xT + e + 1)
                tile_full(pe, gate, i)
                tile_full(pe, up, i)
                gate_up(u, gate, up, used[gate.slot], used[up.slot])

            def outer(e, u, i):
                dn = m.T[3 * u + 2]
                pe.wait_ge(s.hT, b0.hT + e + 1)
                pe.wait_ge(s.y_copied, b0.y_copied + e + 1)
                tile_full(pe, dn, i)
                down(u, dn, used[dn.slot])

            def hidden_turned(e):
                pe.wait_ge(s.hidden, b0.hidden + e + 1)
                turn_h(s.h_turned)

            tokens_in(0, 0)
            inner(0, 0, 0)
            tokens_in(1, 0)
            hidden_turned(0)
            with pe.Fori(0, NE // 2 - 1) as i:
                e = 2 * i + 1
                inner(e, 1, i)
                tokens_in(0, i + 1)
                outer(e - 1, 0, i)
                hidden_turned(e)
                inner(e + 1, 0, i + 1)
                tokens_in(1, i + 1)
                outer(e, 1, i)
                hidden_turned(e + 1)
            last = NE // 2 - 1
            inner(NE - 1, 1, last)
            outer(NE - 2, 0, last)
            hidden_turned(NE - 1)
            outer(NE - 1, 1, last)
            o = m.o
            with pe.If(extra > 0):
                with pe.Fori(0, extra) as i:
                    gate, up, dn = m.T[0:3]
                    pe.wait_ge(o.gathered, (i + 1) * 16)
                    turn_x(0, o.step)
                    pe.wait_ge(o.step, i * STEPS + X_OUT)
                    pe.wait_ge(o.full, (i + 1) * 48)
                    gate_up(0, gate, up, None, o.step)
                    pe.wait_ge(o.step, i * STEPS + HIDDEN)
                    turn_h(o.step)
                    pe.wait_ge(o.step, i * STEPS + H_OUT)
                    down(0, dn, o.down)
                    pe.wait_ge(o.step, i * STEPS + Y_COPIED)

        def combine_order(T):
            return (2, 3, 0, 1)[4 - T:] if T == 4 else (0, 1)

        def act_moe(act, m):
            s, b0, T = m.s, m.b, m.tiles
            for t in range(T):
                act.wait_ge(s.token_turned, b0.token_turned + t + 1)
                if t >= 2:
                    act.wait_ge(s.token_stored[t % 2], b0.token_stored0 + 16)
                act.copy(xn[:, t % 2, :], PS[:, 2 * (t % 2):2 * (t % 2) + 2, :].rearrange("p a b -> p (a b)"))\
                   .then_inc(s.token_copied, 1)
                act.wait_ge(s.token_copied, b0.token_copied + t + 1)
                act.dma_start(tokens_d[t * P:(t + 1) * P, :], xn[:, t % 2, :]).then_inc(s.token_stored[t % 2], 16)
            act.wait_ge(s.group_top, b0.group_top + 1)
            for t in range(T):
                act.activation(m.gexp[:, t, :], m.logits[:, t, 0:EG], ACT.Exp, bias=m.ngtop[:, t:t + 1],
                               accum_out=m.gsum[:, t:t + 1]).then_inc(s.group_exp, 1)
            act.wait_ge(s.expert_gap, b0.expert_gap + 1)
            act.activation(m.ratio, m.gap, ACT.Exp).then_inc(s.expert_exp, 1)
            act.wait_ge(s.routed, b0.routed + 3)
            extra = act.value_load(m.regs[0:1, OVER:OVER + 1], min_val=0, max_val=m.over)
            act.sem_inc(s.y_copied, 2)
            for u in range(2):
                act.sem_inc(s.y_stored[u], 32)

            def x_out(u, done):
                act.copy(XgT[:, u, :], PS[:, 4 + u, :]).then_inc(done, 1)

            def swish_gate(u, done):
                act.activation(swish[CAP:P, :], PS[0:CAP, u, :], ACT.Silu).then_inc(done, 1)

            def y_out(u, blk, done, count, stored):
                act.copy(Yo[:, u, :], PS[:, 2 + u, :]).then_inc(done, 1)
                act.wait_ge(done, count)
                for h in range(2):
                    rows = rows_d[bass.ds(blk * CAP, CAP), h * BANK:(h + 1) * BANK]
                    act.dma_start(rows, Yo[h * CAP:(h + 1) * CAP, u, :]).then_inc(stored, 16)

            def gate_out(u, i):
                tile_used(act, m.T[3 * u], i)
                swish_gate(u, s.swish)

            def rows_out(e, u, i):
                tile_used(act, m.T[3 * u + 2], i)
                act.wait_ge(s.y_stored[u], b0.y_stored0 + (i + 1) * 32)
                y_out(u, e, s.y_copied, b0.y_copied + e + 3, s.y_stored[u])

            gate_out(0, 0)
            with act.Fori(0, NE // 2 - 1) as i:
                gate_out(1, i)
                rows_out(2 * i, 0, i)
                gate_out(0, i + 1)
                rows_out(2 * i + 1, 1, i)
            last = NE // 2 - 1
            gate_out(1, last)
            rows_out(NE - 2, 0, last)
            rows_out(NE - 1, 1, last)
            for u in range(2):
                act.wait_ge(s.y_stored[u], b0.y_stored0 + (NE // 2 + 1) * 32)
            o = m.o
            with act.If(extra > 0):
                with act.Fori(0, extra) as i:
                    act.wait_ge(o.step, i * STEPS + X_TURNED)
                    x_out(0, o.step)
                    act.wait_ge(o.step, i * STEPS + GATE_UP)
                    swish_gate(0, o.step)
                    act.wait_ge(o.down, i + 1)
                    y_out(0, i + NE, o.step, i * STEPS + Y_COPIED, o.y_stored)
                    act.wait_ge(o.y_stored, (i + 1) * 32)
            act.sem_inc(s.stored, 1)
            act.wait_ge(s.weights_ready, b0.weights_ready + 1)
            for n, t in enumerate(combine_order(T)):
                act.wait_ge(s.fetched[n], (b0.fetched0, b0.fetched2)[n // 2] + 32)
                act.activation(fetched[:, n, 0, :], fetched[:, n, 0, :], ACT.Copy, scale=m.wts[:, 0, t:t + 1])\
                   .then_inc(s.weighted, 1)

        def dve_moe(dve, m):
            s, b0, T, n = m.s, m.b, m.tiles, 2 * m.tiles
            step = counts.setdefault("routing", Count(dve, s.dve))

            def do(ins):
                step(ins)
                step.wait()

            def over(a, shape, *axes):
                for x in axes:
                    a = a.unsqueeze(x)
                return a.to_broadcast(shape)

            def flat(a):
                return a.rearrange("p a b -> p (a b)")

            dve.memset(m.prefix[:, 0, :], 0.0)
            do(dve.memset(m.g8, NEG))
            dve.wait_ge(s.logits, b0.logits + 1)
            dve.wait_ge(s.weights, b0.weights + 64)
            do(dve.tensor_tensor(m.logits, PS[:, 4, 0:T * (EG + NE)].rearrange("p (t e) -> p t e", t=T),
                                 over(m.rb, [P, T, EG + NE], 1), ALU.add))
            do(dve.tensor_copy(m.g8[:, :, 0:EG], m.logits[:, :, 0:EG]))
            for t in range(T):
                do(dve.max(m.gtop[:, t, :], m.g8[:, t, :]))
                do(dve.max_index(m.gidx[:, t, :], m.gtop[:, t, :], m.g8[:, t, :]))
            do(dve.tensor_copy(m.gsel, m.gidx[:, :, 0]))
            dve.tensor_scalar(m.ngtop, m.gtop[:, :, 0], -1.0, None, ALU.mult).then_inc(s.group_top, 1)
            shape = [P, T, NE]
            do(dve.tensor_tensor(m.masked, over(C("group"), shape, 1), over(m.gsel, shape, 2), ALU.not_equal))
            do(dve.scalar_tensor_tensor(m.masked, m.masked, NEG, m.logits[:, :, EG:], ALU.mult, ALU.add))
            for t in range(T):
                do(dve.max(m.etop[:, t, :], m.masked[:, t, :]))
                do(dve.max_index(m.eidx[:, t, :], m.etop[:, t, :], m.masked[:, t, :]))
            for j in range(2):
                do(dve.tensor_copy(m.esel[:, j, :], m.eidx[:, :, j]))
            dve.tensor_tensor(m.gap, m.etop[:, :, 1], m.etop[:, :, 0], ALU.subtract).then_inc(s.expert_gap, 1)
            hot = m.hot.rearrange("p j t e -> p (j t) e")
            do(dve.tensor_tensor(hot, over(C("expert"), [P, n, NE], 1), over(flat(m.esel), [P, n, NE], 2),
                                 ALU.is_equal))
            do(dve.tensor_tensor(m.picked, m.hot[:, 0], m.hot[:, 1], ALU.add))
            for t in range(T):
                ins = dve.tensor_tensor(m.prefix[:, t + 1, :], m.prefix[:, t, :], m.picked[:, t, :], ALU.add)
                if t < T - 1:
                    do(ins)
            ins.then_inc(s.picked, 1)
            dve.wait_ge(s.rank, b0.rank + 1)
            do(dve.tensor_copy(m.rank, PS[:, 5, 0:T * NE].rearrange("p (t e) -> p t e", t=T)))
            do(dve.tensor_copy(m.count, PS[:, 5, T * NE:(T + 1) * NE]))
            full_blocks = range(1, T * P // CAP)
            do(dve.tensor_scalar(m.extra, m.count, float(CAP), None, ALU.is_gt))
            for b in full_blocks[1:]:
                do(dve.scalar_tensor_tensor(m.extra, m.count, float(CAP * b), m.extra, ALU.is_gt, ALU.add))
            x = m.extra
            for i in range(5):
                y, d = m.scan[i % 2], 1 << i
                dve.tensor_copy(y[:, 0:d], x[:, 0:d])
                do(dve.tensor_tensor(y[:, d:], x[:, d:], x[:, 0:NE - d], ALU.add))
                x = y
            through = x
            do(dve.tensor_tensor(m.before, through, m.extra, ALU.subtract))
            tmp = m.tmp.rearrange("p j t e -> p (j t) e")
            for j in range(2):
                do(dve.tensor_tensor(m.tmp[:, j], m.hot[:, j], m.rank, ALU.mult))
            do(dve.tensor_reduce(flat(m.pos), tmp, AX, ALU.add))
            do(dve.tensor_tensor(tmp, hot, over(m.before, [P, n, NE], 1), ALU.mult))
            do(dve.tensor_reduce(flat(m.start), tmp, AX, ALU.add))
            pos, start, turn, spill = flat(m.pos), flat(m.start), flat(m.turn_no), flat(m.spill)
            blk, slot, esel = flat(m.blk), flat(m.slot), flat(m.esel)
            do(dve.tensor_scalar(turn, pos, float(CAP), None, ALU.is_ge))
            do(dve.tensor_copy(spill, turn))
            for b in full_blocks[1:]:
                do(dve.scalar_tensor_tensor(turn, pos, float(CAP * b), turn, ALU.is_ge, ALU.add))
            do(dve.scalar_tensor_tensor(blk, start, float(NE - 1), turn, ALU.add, ALU.add))
            do(dve.tensor_tensor(blk, blk, esel, ALU.subtract))
            do(dve.tensor_tensor(blk, blk, spill, ALU.mult))
            do(dve.tensor_tensor(blk, blk, esel, ALU.add))
            do(dve.scalar_tensor_tensor(slot, turn, -float(CAP), pos, ALU.mult, ALU.add))
            do(dve.scalar_tensor_tensor(flat(m.destf), blk, float(CAP), slot, ALU.mult, ALU.add))
            dve.tensor_tensor(m.slot_hot, over(C("slot"), [P, n, CAP], 1), over(slot, [P, n, CAP], 2),
                              ALU.is_equal).then_inc(s.placed, 1)
            do(dve.tensor_tensor(m.blk_hot, over(C("block"), [P, n, NB], 1), over(blk, [P, n, NB], 2),
                                 ALU.is_equal))
            for j in range(2):
                part = m.blk_hot[:, j * T:(j + 1) * T, :]
                ins = dve.tensor_tensor(part, part, over(C("token")[:, 0:T], [P, T, NB], 2), ALU.mult)
                if j:
                    ins.then_inc(s.placed, 1)
            dve.tensor_copy(flat(m.dest), flat(m.destf)).then_inc(s.routed, 1)
            r = slice(0, 1)
            do(dve.tensor_tensor(m.full_before[r], over(through[r], [1, OVER, NE], 1),
                                 C("over")[r].rearrange("p (b e) -> p b e", b=OVER), ALU.is_le))
            do(dve.tensor_reduce(m.regsf[r, 0:OVER], m.full_before[r], AX, ALU.add))
            do(dve.tensor_scalar(m.regsf[r, 0:OVER], m.regsf[r, 0:OVER], float(NE - 1), None, ALU.min))
            do(dve.tensor_copy(m.regsf[r, OVER:OVER + 1], through[r, NE - 1:NE]))
            dve.tensor_copy(m.regs[r], m.regsf[r]).then_inc(s.routed, 1)
            dve.wait_ge(s.ids, b0.ids + 1)
            dve.tensor_copy(m.idx[0:CAP, :], PS[0:CAP, 7, 0:NB]).then_inc(s.routed, 1)
            dve.wait_ge(s.routed, b0.routed + 3)
            dve.wait_ge(s.expert_exp, b0.expert_exp + 1)
            dve.wait_ge(s.group_exp, b0.group_exp + T)
            do(dve.scalar_tensor_tensor(m.den, m.ratio, 1.0, m.gsum, ALU.add, ALU.mult))
            do(dve.reciprocal(m.wts[:, 0, :], m.den))
            do(dve.tensor_tensor(m.wts[:, 1, :], m.wts[:, 0, :], m.ratio, ALU.mult))
            dve.sem_inc(s.weights_ready, 1)
            extra = dve.value_load(m.regs[0:1, OVER:OVER + 1], min_val=0, max_val=m.over)

            def hidden(u, done):
                dve.tensor_tensor(hid[CAP:P, :], PS[CAP:P, u, :], swish[CAP:P, :], ALU.mult).then_inc(done, 1)

            def h_out(done):
                dve.tensor_copy(hidT.rearrange("p a b -> p (a b)"), PS[:, 6, 0:4 * CAP]).then_inc(done, 1)

            def tokens_out(e, u):
                dve.wait_ge(s.x_turned, b0.x_turned + e + 1)
                dve.tensor_copy(XgT[:, u, :], PS[:, 4 + u, :]).then_inc(s.xT, 1)

            def hidden_out(e, u, i):
                dve.wait_ge(s.swish, b0.swish + e + 1)
                tile_used(dve, m.T[3 * u + 1], i)
                hidden(u, s.hidden)
                dve.wait_ge(s.h_turned, b0.h_turned + e + 1)
                h_out(s.hT)

            tokens_out(0, 0)
            tokens_out(1, 1)
            hidden_out(0, 0, 0)
            with dve.Fori(0, NE // 2 - 1) as i:
                tokens_out(2 * i + 2, 0)
                hidden_out(2 * i + 1, 1, i)
                tokens_out(2 * i + 3, 1)
                hidden_out(2 * i + 2, 0, i + 1)
            hidden_out(NE - 1, 1, NE // 2 - 1)
            o = m.o
            with dve.If(extra > 0):
                with dve.Fori(0, extra) as i:
                    dve.wait_ge(o.step, i * STEPS + SWISH)
                    dve.wait_ge(o.step, i * STEPS + GATE_UP)
                    hidden(0, o.step)
                    dve.wait_ge(o.step, i * STEPS + H_TURNED)
                    h_out(o.step)
            dve.wait_ge(second[m.l].s.gate2, second[m.l].b.gate2 + 16 * (T // 2))
            for n, t in enumerate(combine_order(T)):
                res, rows = (hx, cx)[t // 2][:, t % 2, :], fetched[:, n]
                dve.wait_ge(s.weighted, b0.weighted + n + 1)
                do(dve.scalar_tensor_tensor(rows[:, 1, :], rows[:, 1, :], m.wts[:, 1, t:t + 1], rows[:, 0, :],
                                            ALU.mult, ALU.add))
                do(dve.tensor_tensor(rows[:, 1, :], rows[:, 1, :], gates[:, t // 2, :], ALU.mult))
                dve.tensor_tensor(res, res, rows[:, 1, :], ALU.add).then_inc(s.combined, 1)

        def pool_moe(pool, m):
            s, b0, T = m.s, m.b, m.tiles
            pool.dma_start(m.rw[:, :, 0:EG], ins["rt_grp_w_2"][m.l].rearrange("(k p) e -> p k e", p=P))\
                .then_inc(s.weights, 16)
            pool.dma_start(m.rw[:, :, EG:], ins["rt_exp_w_2"][m.l].rearrange("(k p) e -> p k e", p=P))\
                .then_inc(s.weights, 16)
            pool.dma_start(m.rb[:, 0:EG], ins["rt_grp_b_2"][m.l:m.l + 1, :].to_broadcast([P, EG]))\
                .then_inc(s.weights, 16)
            pool.dma_start(m.rb[:, EG:], ins["rt_exp_b_2"][m.l:m.l + 1, :].to_broadcast([P, NE]))\
                .then_inc(s.weights, 16)
            for u in range(2):
                pool.wait_ge(s.token_stored[u], b0.token_stored0 + 16 * (T // 2))
            pool.wait_ge(s.routed, b0.routed + 3)
            extra = pool.value_load(m.regs[0:1, OVER:OVER + 1], min_val=0, max_val=m.over)

            def gather(u, blk, done):
                pool.indirect_dma_start(out=Xg[0:CAP, u, :], out_offset=None, in_=tokens_d,
                                        in_offset=bass.IndirectOffsetOnAxis(ap=m.idx[0:CAP, blk:blk + 1], axis=0))\
                    .then_inc(done, 16)

            for e in range(NE):
                if e >= 2:
                    pool.wait_ge(s.x_turned, b0.x_turned + e - 1)
                gather(e % 2, e, s.gathered[e % 2])
            pool.wait_ge(s.x_turned, b0.x_turned + NE)
            o = m.o
            for i in range(m.over):
                with pool.If(extra > i):
                    gather(0, NE + i, o.gathered)
                    pool.wait_ge(o.step, i * STEPS + X_TURNED)
            pool.wait_ge(s.stored, b0.stored + 1)
            for n, t in enumerate(combine_order(T)):
                for j in range(2):
                    pool.indirect_dma_start(out=fetched[:, n, j, :], out_offset=None, in_=rows_d,
                                            in_offset=bass.IndirectOffsetOnAxis(ap=m.dest[:, j, t:t + 1], axis=0))\
                        .then_inc(s.fetched[n], 16)

        cx = area(8192, 2, D)
        qT2 = area(10240, 4, SEQ + CTX)
        kT2 = area(12288, 2, SEQ + CTX)
        v2 = area(13312, 4, P)
        W2 = 15872
        rope_bufs = dict(normed=area(W2, 3, BANK), squares=area(W2 + 1536, 2, BANK),
                         rotated=xn[:, :, :].rearrange("p a b -> p (a b)")[:, 0:3 * BANK]
                         .rearrange("p (a b) -> p a b", a=3))
        rope_tab = area(W2 + 2560, 2, 2, 2 * HD)
        rope_src = area(W2 + 3072, 2, 2 * HD)
        rope_gain = area(W2 + 3328, 2, HD)
        gates = area(10240, 2, D)
        bufs2 = dict(logits=area(W2 + 2048, 2, BANK), probs=area(W2, 2, BANK), probsT=area(W2 + 1024, 2, BANK))

        def shift_of(l, j, which):
            c = l * 96 + j * 48 + 24 * which
            return modT[:, c:c + KD]

        def gain_of(l, j, which):
            c = ((l * 2 + j) * 2 + which) * KD
            return modg[:, c:c + KD]

        second = [Record(l=l) for l in range(2)]
        for L in second:
            l = L.l
            L.s, L.b = shared("layer", rope_loaded=48, rope_ready=6, gate1=16 * (2 - l), gate2=16 * (2 - l))
        s_mod = sems("mod", "rows turned copied gain")
        s_cx = sem("ctx_loaded")

        mod_ready = [(s_mod.copied, 1), (s_mod.gain, 8)]

        L = second[0]
        L.nc = norm_stage(cx, XT[:, :, SEQ:SEQ + CTX], gain_of(0, 1, 0), shift_of(0, 1, 0),
                          [(s_cx, 16)] + mod_ready)
        L.nx = norm_stage(hx, XT[:, :, 0:SEQ], gain_of(0, 0, 0), shift_of(0, 0, 0), f_b.done + mod_ready)
        Tq, Tk = T_ab[0:2]

        def attention_units(Tq, Tk, q_tiles, qg, kg):
            us = []
            for t in range(q_tiles):
                rope = (rope_tab[:, 0, 0, t * HD:(t + 1) * HD], rope_tab[:, 0, 1, t * HD:(t + 1) * HD]) if t < 2 else None
                us.append(unit(Tq, t, qk=heads(8, qT2[:, :, t * P:(t + 1) * P], rope=rope,
                                               gain=None if rope else vcol(qg))))
            for t in range(4):
                rope = (rope_tab[:, 1, 0, t * HD:(t + 1) * HD], rope_tab[:, 1, 1, t * HD:(t + 1) * HD]) if t < 2 else None
                us.append(unit(Tk, t, width=256, qk=heads(2, kT2[:, :, t * P:(t + 1) * P], rope=rope, dup=2,
                                                          gain=None if rope else vcol(kg)), v=v2[:, t, :], v_src=P))
            return us

        L.q = qkv_stage(XT, attention_units(Tq, Tk, 4, "q_norm_a_2", "k_norm_a_2"), **rope_bufs)

        def grouped_steps(tiles, o, keys_of, bias_of, sink_of):
            steps = []
            for h in range(8):
                half, pair, kv = slice((h % 2) * HD, (h % 2) * HD + HD), h // 2, h // 4
                for t in range(tiles):
                    k0, k1 = keys_of(t)
                    steps.append(Record(
                        scores=[(0, qT2[half, pair, t * P:(t + 1) * P], kT2[half, kv, k0:k1])], width=k1 - k0,
                        values=[v2[:, kt, kv * HD:(kv + 1) * HD] for kt in range(k0 // P, k1 // P)],
                        bias=bias_of(t), bias_ready=None, sink=sink_of(h), out=o[:, t, h * HD:(h + 1) * HD]))
            return steps

        o_ab = area(13824, 4, BANK)
        glu = area(4096, 4, 2, SEQ + TAPS - 1)
        sig = area(13824, 2, BANK)
        conv = area(0, 4, 2, SEQ)
        conv2 = area(0, 4, BANK)
        conv_sq = area(2048, 4, BANK)
        MT = area(4096, 8, BANK)
        s_glu = sems("glu", "product sigmoid out zeroed")
        s_conv = sems("conv", "w_rows w_turned w_ready taps product taps_last mean centred squared var root inverse scaled out")
        glu_done = [(s_glu.out, 4)]
        conv_done = [(s_conv.taps, 2 * TAPS), (s_conv.taps_last, 2 * TAPS)]
        L.at = attention(grouped_steps(4, o_ab, lambda t: (0, 512) if t < 2 else (SEQ, SEQ + CTX),
                                               lambda t: None, lambda h: None), L.q.done + glu_done, False, bufs2)
        L.tn = turn_stage(o_ab, MT, 4, BANK, L.at.done + conv_done)

        def out_units(T, tiles):
            return [Record(tile=T[h], t=t, terms=[(k, w8(T[h])[:, k, :]) for k in range(8)],
                            res=(hx, cx)[t // 2][:, t % 2, h * BANK:(h + 1) * BANK],
                            gate=gates[:, t // 2, h * BANK:(h + 1) * BANK])
                    for h in range(2) for t in range(tiles)]

        L.pr = proj_stage(MT, out_units(T_abo, 4), L.tn.done + [(s_conv.out, 4)])
        L.nc2 = norm_stage(cx, XT[:, :, SEQ:SEQ + CTX], gain_of(0, 1, 1), shift_of(0, 1, 1), L.pr.done)
        L.nx2 = norm_stage(hx, XT[:, :, 0:SEQ], gain_of(0, 0, 1), shift_of(0, 0, 1), L.pr.done)

        L = second[1]
        L.nc = norm_stage(cx, XT[:, :, SEQ:SEQ + CTX], gain_of(1, 1, 0), shift_of(1, 1, 0), [])
        L.nx = norm_stage(hx, XT[:, :, 0:SEQ], gain_of(1, 0, 0), shift_of(1, 0, 0), [])
        pooled_in = area(7168, 2, BANK)
        units = attention_units(T_cd[0], T_cd[1], 2, "q_norm_c_2", "k_norm_c_2")
        units += [unit(T_cd[2], t, v=pooled_in[:, t, :]) for t in range(2)]
        L.q = qkv_stage(XT, units, **rope_bufs)
        o_cd = area(13824, 2, BANK)
        band = area(6144, 2, BANK)
        pool_tab = area(8192, 2, len(POOLS), SEQ)
        pool_w = area(14848, 4, P)
        pooled = xn[:, :, :].rearrange("p a b -> p (a b)")[:, 0:4 * SEQ].rearrange("p (a b) -> p a b", a=4)
        MT1 = area(4096, 8, SEQ)
        s_band = sems("band", "loaded table weights sinks")
        s_pool = sems("pool", "mean copied mixed out")
        sinks = small[:, 128:136]
        L.at = attention(grouped_steps(2, o_cd, lambda t: (0, 512), lambda t: band[:, t, :],
                                               lambda h: sinks[:, h:h + 1]),
                         L.q.done + [(s_band.loaded, 16), (s_band.sinks, 16)], True, bufs2)
        L.tn = turn_stage(o_cd, MT1, 2, BANK, L.at.done)
        L.pr = proj_stage(MT1, out_units(T_cdo, 2), L.tn.done + [(s_pool.out, 4)])
        L.nx2 = norm_stage(hx, XT[:, :, 0:SEQ], gain_of(1, 0, 1), shift_of(1, 0, 1), L.pr.done)

        Xg = area(4096, 2, D)
        XgT = area(6144, 2, BANK)
        swish = area(7168, BANK)
        hid = area(7680, BANK)
        hidT = area(12288, 4, CAP)
        Yo = area(12544, 2, BANK)
        RT = 13568

        def moe_stage(l, tiles, T):
            m = Record(l=l, tiles=tiles, T=T, over=blocks_most(tiles * P) - NE)
            m.blocks = NE + m.over
            T2, E = tiles // 2 * 16, NE // 2 * 16
            m.s, m.b = shared("moe", token_turned=tiles, token_copied=tiles, token_stored0=T2, token_stored1=T2,
                              weights=64, logits=1, dve=0, group_top=1, group_exp=tiles, expert_gap=1, expert_exp=1,
                              picked=1, rank=1, placed=2, ids=1, routed=3, gathered0=E, gathered1=E,
                              x_turned=NE, xT=NE, swish=NE, hidden=NE, h_turned=NE, hT=NE, y_copied=NE + 2,
                              y_stored0=2 * E + 32, y_stored1=2 * E + 32, stored=1, combined=tiles,
                              fetched0=32, fetched1=32, fetched2=16 * (tiles - 2), fetched3=16 * (tiles - 2),
                              weighted=tiles, weights_ready=1)
            m.o = sems(f"over{l}", "full down gathered step y_stored")
            m.done = [(m.s.combined, m.b.combined + tiles)]
            m.s.gathered, m.s.y_stored = (m.s.gathered0, m.s.gathered1), (m.s.y_stored0, m.s.y_stored1)
            m.s.fetched = (m.s.fetched0, m.s.fetched1, m.s.fetched2, m.s.fetched3)
            m.s.token_stored = (m.s.token_stored0, m.s.token_stored1)
            n, col = 2 * tiles, [RT]

            def take(*shape, dt=None):
                size = int(np.prod(shape))
                a = area(col[0], *shape)
                col[0] += size
                return a if dt is None else a.bitcast(dt)
            m.rw, m.rb = take(KD, EG + NE), take(EG + NE)
            m.logits = take(tiles, EG + NE)
            m.g8, m.gtop, m.gidx = take(tiles, 8), take(tiles, 8), take(tiles, 8, dt=U32)
            m.gsel, m.ngtop, m.gsum, m.gexp = take(tiles), take(tiles), take(tiles), take(tiles, EG)
            m.masked, m.etop, m.eidx = take(tiles, NE), take(tiles, 8), take(tiles, 8, dt=U32)
            m.esel, m.gap, m.ratio, m.den, m.wts = take(2, tiles), take(tiles), take(tiles), take(tiles), take(2, tiles)
            m.hot, m.picked, m.prefix = take(2, tiles, NE), take(tiles, NE), take(tiles + 1, NE)
            m.rank, m.count = take(tiles, NE), take(NE)
            m.extra, m.scan = take(NE), [take(NE), take(NE)]
            m.before = take(NE)
            m.tmp = take(2, tiles, NE)
            m.pos, m.start, m.turn_no = take(2, tiles), take(2, tiles), take(2, tiles)
            m.spill, m.blk, m.slot = take(2, tiles), take(2, tiles), take(2, tiles)
            m.destf, m.dest = take(2, tiles), take(2, tiles, dt=U32)
            m.slot_hot, m.blk_hot = take(n, CAP), take(n, NB)
            m.idx = take(NB, dt=U32)
            m.full_before = take(OVER, NE)
            m.regsf, m.regs = take(OVER + 1), take(OVER + 1, dt=I32)
            assert col[0] <= ARENA, col[0]
            return m

        moes = [moe_stage(0, 4, T_moe[0]),
                moe_stage(1, 2, T_moe[1])]
        second[1].nc.ready = [(moes[0].s.combined, moes[0].b.combined + 2)]
        second[1].nx.ready = moes[0].done
        fetched = area(0, 4, 2, D)

        modrows = area(13824, 2, P)
        convrows = arena[0:TAPS, 14848:14848 + BANK]
        s_out = sem("out_stored")
        vrows = arena[0:VROWS, 11264:11264 + P]
        table = arena[0:BUCKETS, 11400:11400 + A_HEADS]
        diag = arena[0:BUCKETS, 16000:16000 + 3 * TOEP]
        browA = arena[0:A_HEADS, 18432:18432 + TOEP]
        browB = arena[0:B_HEADS, 18432 + TOEP:18432 + 2 * TOEP]
        n_small = [0]

        block = ctx.enter_context(nc.Block())

        def tap_product(c, k):
            return conv_sq[:, 2 * (c - 2) + k % 2, :].rearrange("p (s t) -> p s t", s=2)

        @block.sync
        def _(sp):
            def load(tile, src, i=0):
                assert tile.first or isinstance(i, int)
                if tile.first:
                    sp.wait_ge(used[tile.slot], use(tile, i))
                kk, n = src.shape[1], src.shape[2]
                sp.dma_start(ring[:, tile.slot, 0:kk * n].rearrange("p (k n) -> p k n", k=kk), src)\
                    .then_inc(full[tile.slot], 16)

            def columns(w, n, width=BANK):
                c = slice(n, n + width) if isinstance(n, int) else bass.ds(n, width)
                return w[:, c].rearrange("(k p) n -> p k n", p=P)

            def ffn_loads(l, T):
                w1, w2, mw = ins["ffn_w1"][l], ins["ffn_w2"][l], ins["mod_w_2"][l]

                def rows(j):
                    c = slice(j * BANK, (j + 1) * BANK) if isinstance(j, int) else bass.ds(j * BANK, BANK)
                    return w2[c, :].rearrange("(p k) n -> p k n", k=4)
                load(T.head[0], columns(w1, 0))
                load(T.head[1], columns(w1, BANK))
                load(T.head[2], rows(0))
                with sp.Fori(0, 3) as i:
                    for h in range(2):
                        j, m = 2 * i + 2 + h, 4 * i + 2 * h
                        load(T.body[4 * h], columns(w1, j * BANK), i)
                        load(T.body[4 * h + 1], columns(mw, m * BANK), i)
                        load(T.body[4 * h + 2], columns(mw, (m + 1) * BANK), i)
                        load(T.body[4 * h + 3], rows(j - 1), i)
                load(T.tail[0], rows(FF_TILES - 1))

            sp.dma_start(hx[:, :, :], ins["x"][0].rearrange("(t p) d -> p t d", p=P)).then_inc(s_x, 16)
            sp.dma_start(const[:, :], ins["shape_table"]).then_inc(s_const, 16)
            load(T_aqkv[0], columns(ins["a_w_qkv"][0], 0))
            sp.wait_ge(s_diag, 32)
            for n in range(1, 9):
                load(T_aqkv[n], columns(ins["a_w_qkv"][0], n * BANK))
            load(T_awo[0], ins["a_w_o"][0].rearrange("(k p) n -> p k n", p=P))
            ffn_loads(0, T_ffn[0])
            for n in range(6):
                load(T_bqkv[n], columns(ins["b_w_qkv"][0], n * BANK))
            for n in range(2):
                load(T_bwo[n], columns(ins["b_w_o"][0], n * BANK))
            ffn_loads(1, T_ffn[1])
            ab, cd = ins["w_in_ab_2"][0], ins["w_in_cd_2"][0]
            load(T_ab[0], columns(ab, 0))
            load(T_ab[1], columns(ab, 512, 256))
            load(T_ab[2], columns(ab, 768))
            load(T_ab[3], columns(ab, 1280))
            for n in range(2):
                load(T_abo[n], columns(ins["w_out_ab_2"][0], n * BANK))

            def expert(w, l, e, k):
                return w[l, bass.ds(e, 1), :, :].rearrange("a (p k) n -> p (a k) n", k=k)

            def moe_loads(m):
                l = m.l
                names = (("ex_gate_2", KD), ("ex_up_2", KD), ("ex_down_2", 4))
                with sp.Fori(0, NE // 2) as i:
                    for u in range(2):
                        for n, (name, k) in enumerate(names):
                            load(m.T[3 * u + n], expert(ins[name], l, 2 * i + u, k), i)
                sp.wait_ge(m.s.routed, m.b.routed + 3)
                extra = sp.value_load(m.regs[0:1, OVER:OVER + 1], min_val=0, max_val=m.over)
                for t in m.T[0:3]:
                    sp.wait_ge(used[t.slot], t.first + t.per * (NE // 2))

                for i in range(m.over):
                    with sp.If(extra > i):
                        e = sp.value_load(m.regs[0:1, i:i + 1], min_val=0, max_val=NE - 1)
                        for n, (name, k) in enumerate(names):
                            src = expert(ins[name], l, e, k)
                            sp.dma_start(ring[:, m.T[n].slot, :].rearrange("p (k n) -> p k n", k=k), src)\
                              .then_inc(m.o.full, 16)
                        sp.wait_ge(m.o.full, 48 * (i + 1))
                        sp.wait_ge(m.o.down, i + 1)

            moe_loads(moes[0])
            for n in range(4):
                sp.wait_ge(moes[0].s.fetched[n], 32)
            load(T_cd[0], columns(cd, 0))
            load(T_cd[1], columns(cd, 512, 256))
            load(T_cd[2], columns(cd, 768))
            for n in range(2):
                load(T_cdo[n], columns(ins["w_out_cd_2"][0], n * BANK))
            moe_loads(moes[1])

        @block.tensor
        def _(pe):
            pe.wait_ge(s_const, 16)
            pe_norm(pe, n_a1)
            pe.wait_ge(s_vrows, 16 * N_VLOADS)
            pe.transpose(PS[:, 4, 0:VROWS], vrows, ident[0:VROWS, 0:VROWS]).then_inc(s_vT, 1)
            pe.wait_ge(s_diag, 32)
            pe.matmul(PS[0:A_HEADS, 5, 0:TOEP], table, diag[:, 0:TOEP], start=True, stop=True).then_inc(s_brow, 1)
            at(pe, *n_a1.done, (s_bsb, 2), (s_vec, 1))
            pe_qkv(pe, q_a)
            pe_attention(pe, at_a)
            pe_turn(pe, tn_a)
            pe_proj(pe, pr_a)
            pe_norm(pe, n_a2)
            pe.wait_ge(s_silu, 2)
            pe_ffn(pe, f_a)
            pe_norm(pe, n_b1)
            at(pe, *n_b1.done)
            pe_qkv(pe, q_b)
            pe_attention(pe, at_b)
            pe_turn(pe, tn_b)
            pe_proj(pe, pr_b)
            pe_norm(pe, n_b2)
            pe_ffn(pe, f_b)

            L0, L1 = second
            at(pe, *f_b.done)
            pe.wait_ge(s_mod.rows, 32)
            for l in range(2):
                mm = pe.transpose(PS[:, 4, l * 96:(l + 1) * 96], modrows[0:96, l, :], ident[0:96, 0:96])
            mm.then_inc(s_mod.turned, 1)
            pe.wait_ge(s_conv.w_rows, 16)
            for c in range(4):
                mm = pe.transpose(PS[:, 5, c * TAPS:(c + 1) * TAPS], convrows[:, c * P:(c + 1) * P],
                                  ident[0:TAPS, 0:TAPS])
            mm.then_inc(s_conv.w_turned, 1)
            pe_norm(pe, L0.nc)
            at(pe, *L0.nc.done)
            pe_norm(pe, L0.nx)
            at(pe, *L0.nx.done)
            at(pe, (s_mod.copied, 1), (s_conv.w_ready, 1))
            pe_qkv(pe, L0.q)
            at(pe, *L0.q.done)
            for c in range(4):
                if c >= 2:
                    pe.wait_ge(s_glu.out, c - 1)
                for n, tile in enumerate(T_ab[2:4]):
                    if c == 0:
                        tile_full(pe, tile)
                    for k in range(KD):
                        mm = pe.matmul(PS[:, 4 + 2 * (c % 2) + n, :], w8(tile)[:, k, c * P:(c + 1) * P], XT[:, k, :],
                                       start=(k == 0), stop=(k == KD - 1))
                    mm.then_inc(used[tile.slot] if c == 3 else s_glu.product, 1)
            pe_attention(pe, L0.at)
            at(pe, *L0.at.done)
            at(pe, *conv_done)
            pe.wait_ge(s_set, 2)
            for c in range(4):
                mm = pe.matmul(PS[:, 0, :], ones, conv2[:, c, :], start=(c == 0), stop=(c == 3))
            mm.then_inc(s_conv.mean, 1)
            pe.wait_ge(s_conv.squared, 4)
            for c in range(4):
                mm = pe.matmul(PS[:, 1, :], ones, conv_sq[:, c, :], start=(c == 0), stop=(c == 3))
            mm.then_inc(s_conv.var, 1)
            at(pe, (s_conv.inverse, 1))
            pe_turn(pe, L0.tn)
            at(pe, *L0.tn.done)
            pe_proj(pe, L0.pr)
            at(pe, *L0.pr.done)
            pe_norm(pe, L0.nc2)
            at(pe, *L0.nc2.done)
            pe_norm(pe, L0.nx2)
            at(pe, *L0.nx2.done)
            pe_moe(pe, moes[0])

            pe_norm(pe, L1.nc)
            at(pe, *L1.nc.done)
            pe_norm(pe, L1.nx)
            at(pe, *L1.nx.done)
            pe_qkv(pe, L1.q)
            at(pe, *L1.q.done)
            pe_attention(pe, L1.at)
            at(pe, *L1.at.done)
            at(pe, (s_band.table, 16), (s_band.weights, 16))
            for g in range(4):
                for t in range(2):
                    mm = pe.matmul(PS[:, g // 2, (g % 2) * SEQ:(g % 2 + 1) * SEQ],
                                   pooled_in[:, t, g * P:(g + 1) * P], pool_tab[:, t, g, :],
                                   start=(t == 0), stop=(t == 1))
            mm.then_inc(s_pool.mean, 1)
            pe.wait_ge(s_pool.copied, 1)
            for g in range(4):
                mm = pe.matmul(PS[:, 2 + g // 2, (g % 2) * SEQ:(g % 2 + 1) * SEQ], pool_w[:, g, :], pooled[:, g, :],
                               start=True, stop=True)
            mm.then_inc(s_pool.mixed, 1)
            at(pe, (s_pool.out, 4))
            pe_turn(pe, L1.tn)
            at(pe, *L1.tn.done)
            pe_proj(pe, L1.pr)
            at(pe, *L1.pr.done)
            pe_norm(pe, L1.nx2)
            at(pe, *L1.nx2.done)
            pe_moe(pe, moes[1])


        @block.scalar
        def _(act):
            def vload(dst, src):
                act.dma_start(dst, src).then_inc(s_vrows, 16)
                n_small[0] += 1
            for name, row in VEC.items():
                a = ins[name]
                flat = a.rearrange("a b -> (a b)") if len(a.shape) == 2 else a
                if flat.shape[0] == HD:
                    for half in range(2):
                        vload(vrows[row:row + 1, half * HD:(half + 1) * HD], flat.rearrange("(r c) -> r c", r=1))
                else:
                    n = flat.shape[0] // P
                    vload(vrows[row:row + n, :], flat.rearrange("(r c) -> r c", c=P))
            assert n_small[0] == N_VLOADS
            act.dma_start(diag, ins["shape_diag"]).then_inc(s_diag, 16)
            act.dma_start(table, ins["rel_bias"]).then_inc(s_diag, 16)
            act.wait_ge(s_const, 16)
            act_norm(act, n_a1, table_ready=[(s_vec, 1)])
            act.wait_ge(s_set, 1)
            for j, name in enumerate(("c_2", "c_ctx_2")):
                act.activation(silu_c[:, :, j], vcol(name, 0, KD), ACT.Silu).then_inc(s_silu, 1)
            act_qkv(act, q_a)
            act_attention(act, at_a)
            act_turn(act, tn_a)
            act_norm(act, n_a2)
            act_ffn(act, f_a)
            act_norm(act, n_b1)
            act_qkv(act, q_b)
            act_attention(act, at_b)
            act_turn(act, tn_b)
            act_norm(act, n_b2)
            act_ffn(act, f_b)

            L0, L1 = second
            act_norm(act, L0.nc)
            at(act, L0.nc.turned)
            act_norm(act, L0.nx)
            act_qkv(act, L0.q)
            for c in range(4):
                at(act, (used[T_ab[3].slot], T_ab[3].first + 1) if c == 3 else (s_glu.product, 2 * c + 2))
                if c >= 2:
                    act.wait_ge(s_glu.out, c - 1)
                act.activation(sig[:, c % 2, :], PS[:, 5 + 2 * (c % 2), :], ACT.Sigmoid).then_inc(s_glu.sigmoid, 1)
            at(act, (s_glu.out, 4), (s_conv.w_ready, 1), (used[T_ab[3].slot], T_ab[3].first + 1))

            def tap_products(k):
                if not 1 <= k < TAPS:
                    return
                for c in (2, 3):
                    if k >= 3:
                        act.wait_ge(s_conv.taps_last, 2 * (k - 2) + c - 1)
                    act.activation(tap_product(c, k), glu[:, c, :, k:k + SEQ], ACT.Copy, scale=convw[:, c, k:k + 1])\
                       .then_inc(s_conv.product, 1)

            act_attention(act, L0.at, between=tap_products)
            for c in range(4):
                act.wait_ge(s_conv.centred, c + 1)
                act.activation(conv_sq[:, c, :], conv2[:, c, :], ACT.Square).then_inc(s_conv.squared, 1)
            act.wait_ge(s_conv.var, 1)
            root(act, conv_sq[:, 1, :], PS[:, 1, :], BANK).then_inc(s_conv.root, 1)
            for c in range(4):
                act.wait_ge(s_conv.scaled, c + 1)
                act.activation(MT[:, 4 + c, :], conv2[:, c, :], ACT.Silu, bias=vcol("conv_ln_b_2", c),
                               scale=vcol("conv_ln_g_2", c)).then_inc(s_conv.out, 1)
            act_turn(act, L0.tn)
            act_norm(act, L0.nc2)
            at(act, L0.nc2.turned)
            act_norm(act, L0.nx2)
            act_moe(act, moes[0])

            act_norm(act, L1.nc)
            at(act, L1.nc.turned)
            act_norm(act, L1.nx)
            act_qkv(act, L1.q)
            act_attention(act, L1.at)
            act.wait_ge(s_pool.mean, 1)
            act.copy(pooled.rearrange("p a b -> p (a b)"), PS[:, 0:2, :].rearrange("p a b -> p (a b)"))\
               .then_inc(s_pool.copied, 1)
            act.wait_ge(s_pool.mixed, 1)
            for g in range(4):
                act.activation(MT1[:, 4 + g, :], PS[:, 2 + g // 2, (g % 2) * SEQ:(g % 2 + 1) * SEQ], ACT.Copy,
                               scale=vcol("pool_scale_2", g)).then_inc(s_pool.out, 1)
            act_turn(act, L1.tn)
            act_norm(act, L1.nx2)
            act_moe(act, moes[1])


        @block.vector
        def _(dve):
            dve.memset(silu_c[:, :, :], 0.0).then_inc(s_set, 1)
            dve.memset(ones, 1.0).then_inc(s_set, 1)

            def vectors():
                dve.wait_ge(s_vT, 1)
                dve.tensor_copy(vec[:, :], PS[:, 4, 0:VROWS]).then_inc(s_vec, 1)
                dve.wait_ge(s_vec, 1)
            dve_norm(dve, n_a1, between=vectors)
            dve.wait_ge(s_brow, 1)
            dve.tensor_tensor(browA, PS[0:A_HEADS, 5, 0:TOEP], diag[0:A_HEADS, TOEP:2 * TOEP], ALU.add)\
               .then_inc(s_bsb, 1)
            dve.tensor_tensor(browB, PS[0:B_HEADS, 5, 0:TOEP], diag[0:B_HEADS, 2 * TOEP:3 * TOEP], ALU.add)\
               .then_inc(s_bsb, 1)
            dve_qkv(dve, q_a)
            dve_attention(dve, at_a)
            dve.wait_ge(at_a.done[0][0], at_a.done[0][1])
            dve.memset(zeros, 0.0).then_inc(s_zero, 1)
            dve_proj(dve, pr_a)
            dve_norm(dve, n_a2)
            dve_ffn(dve, f_a)
            dve_norm(dve, n_b1)
            dve_qkv(dve, q_b)
            dve_attention(dve, at_b)
            dve_proj(dve, pr_b)
            dve_norm(dve, n_b2)
            dve_ffn(dve, f_b)

            L0, L1 = second
            dve.wait_ge(s_mod.turned, 1)
            dve.tensor_copy(modT[:, :], PS[:, 4, 0:192]).then_inc(s_mod.copied, 1)
            dve.wait_ge(s_mod.copied, 1)
            for l in range(2):
                for j in range(2):
                    for which in range(2):
                        sc = l * 96 + j * 48 + 24 * which + 8
                        dve.scalar_tensor_tensor(gain_of(l, j, which), modT[:, sc:sc + KD], 1.0,
                                                 vcol(("ln1_g_2", "ln2_g_2")[which], l * KD, KD), ALU.add, ALU.mult)\
                           .then_inc(s_mod.gain, 1)
            dve.wait_ge(s_conv.w_turned, 1)
            dve.tensor_copy(convw, PS[:, 5, 0:4 * TAPS].rearrange("p (c k) -> p c k", c=4)).then_inc(s_conv.w_ready, 1)

            def rope_tables(L):
                dve.wait_ge(L.s.rope_loaded, L.b.rope_loaded + 48)
                for v in range(2):
                    gain = rope_gain[:, v, :]
                    tab = rope_tab[:, v, 0, :].rearrange("p (t d) -> p t d", t=2)
                    dve.tensor_tensor(tab, rope_src[:, 0, :].rearrange("p (t d) -> p t d", t=2),
                                      gain.unsqueeze(1).to_broadcast([P, 2, HD]), ALU.mult).then_inc(L.s.rope_ready, 1)
                    tab = rope_tab[:, v, 1, :].rearrange("p (t d) -> p t d", t=2)
                    src = rope_src[:, 1, :].rearrange("p (t d) -> p t d", t=2)
                    for a, b in ((0, HD // 2), (HD // 2, 0)):
                        dve.tensor_tensor(tab[:, :, a:a + HD // 2], src[:, :, a:a + HD // 2],
                                          gain[:, b:b + HD // 2].unsqueeze(1).to_broadcast([P, 2, HD // 2]),
                                          ALU.mult).then_inc(L.s.rope_ready, 1)

            rope_tables(L0)
            dve.wait_ge(s_mod.gain, 8)
            dve_norm(dve, L0.nc)
            dve_norm(dve, L0.nx)
            dve.wait_ge(L0.s.rope_ready, L0.b.rope_ready + 6)
            at(dve, L0.nx.turned)
            dve_qkv(dve, L0.q)
            dve.memset(glu, 0.0).then_inc(s_glu.zeroed, 1)
            dve.wait_ge(s_glu.zeroed, 1)
            for c in range(4):
                dve.wait_ge(s_glu.sigmoid, c + 1)
                at(dve, (used[T_ab[2].slot], T_ab[2].first + 1) if c == 3 else (s_glu.product, 2 * c + 1))
                dve.tensor_tensor(glu[:, c, :, TAPS // 2:TAPS // 2 + SEQ],
                                  PS[:, 4 + 2 * (c % 2), :].rearrange("p (s t) -> p s t", s=2),
                                  sig[:, c % 2, :].rearrange("p (s t) -> p s t", s=2), ALU.mult)\
                   .then_inc(s_glu.out, 1)
            dve.wait_ge(s_glu.out, 4)
            dve.wait_ge(s_conv.w_ready, 1)
            at(dve, (used[T_ab[3].slot], T_ab[3].first + 1))

            def tap(k):
                if k >= TAPS:
                    return
                for c in range(2):
                    src, dst = glu[:, c, :, k:k + SEQ], conv[:, c, :, :]
                    if k == 0:
                        dve.tensor_scalar(dst, src, convw[:, c, 0:1], vcol("conv_b_2", c), ALU.mult, ALU.add)\
                           .then_inc(s_conv.taps, 1)
                    else:
                        dve.wait_ge(s_conv.taps, 2 * (k - 1) + c + 1)
                        dve.scalar_tensor_tensor(dst, src, convw[:, c, k:k + 1], dst, ALU.mult, ALU.add)\
                           .then_inc(s_conv.taps, 1)
            dve_attention(dve, L0.at, between=tap)
            dve.wait_ge(s_conv.mean, 1)
            at(dve, *conv_done)
            for c in range(4):
                dve.scalar_tensor_tensor(conv2[:, c, :], PS[:, 0, :], -1.0 / BANK, conv2[:, c, :], ALU.mult, ALU.add)\
                   .then_inc(s_conv.centred, 1)
            dve.wait_ge(s_conv.root, 1)
            dve.reciprocal(conv_sq[:, 2, :], conv_sq[:, 1, :]).then_inc(s_conv.inverse, 1)
            dve.wait_ge(s_conv.inverse, 1)
            for c in range(4):
                dve.tensor_tensor(conv2[:, c, :], conv2[:, c, :], conv_sq[:, 2, :], ALU.mult)\
                   .then_inc(s_conv.scaled, 1)
            dve.wait_ge(L0.s.gate1, L0.b.gate1 + 32)
            dve_proj(dve, L0.pr)
            at(dve, *L0.pr.done)
            dve_norm(dve, L0.nc2)
            dve_norm(dve, L0.nx2)
            dve_moe(dve, moes[0])

            rope_tables(L1)
            dve_norm(dve, L1.nc)
            dve_norm(dve, L1.nx)
            dve.wait_ge(L1.s.rope_ready, L1.b.rope_ready + 6)
            at(dve, L1.nx.turned)
            dve_qkv(dve, L1.q)
            dve_attention(dve, L1.at)
            dve.wait_ge(L1.s.gate1, L1.b.gate1 + 16)
            dve_proj(dve, L1.pr)
            at(dve, *L1.pr.done)
            dve_norm(dve, L1.nx2)
            dve_moe(dve, moes[1])


        @block.gpsimd
        def _(pool):
            pool.wait_ge(s_bsb, 2)
            for rows, dst in ((browA, bias_a), (browB, bias_b)):
                src = bass.AP(tensor=rows.tensor, offset=rows.offset + P - 1,
                              ap=[[ARENA, dst.shape[0]], [-1, P], [1, SEQ]])
                pool.dma_start(dst, src).then_inc(s_bd, 16)

            def bias_tiles(a, rows, n, heads_each, head_step, steps_each):
                for i in range(n):
                    if i >= 2:
                        pool.wait_ge(a.s.biased, a.b.biased + steps_each * (i - 1))
                    elif a is at_b:
                        at(pool, *at_a.done)
                    first = i * (1 if head_step > 1 else heads_each)
                    src = rows[first:first + head_step * (heads_each - 1) + 1:head_step].rearrange("g p k -> p g k")
                    pool.dma_start(biasbuf[:, i % 2, 0:heads_each, :], src).then_inc(s_bias[i % 2], 16)

            pool.wait_ge(s_bd, 32)
            at(pool, *q_a.done)
            bias_tiles(at_a, bias_a, GH, NG, GH, 2)
            pool.wait_ge(s_zero, 1)
            for r in range(NE * CAP, YROWS, P):
                n = min(P, YROWS - r)
                pool.dma_start(rows_d[r:r + n, :], zeros[0:n, :]).then_inc(s_zeroed, 16)
            pool_ffn(pool, f_a)
            bias_tiles(at_b, bias_b, B_HEADS // 2, 2, 1, 4)
            L0, L1 = second

            def rope_loads(L, q_name, k_name):
                pool.dma_start(rope_src.rearrange("p a b -> p (a b)"), ins["shape_rope"]).then_inc(L.s.rope_loaded, 16)
                for v, name in enumerate((q_name, k_name)):
                    pool.dma_start(rope_gain[:, v, :], ins[name][0:1, :].to_broadcast([P, HD]))\
                        .then_inc(L.s.rope_loaded, 16)

            def gate_loads(L, which, streams, sem):
                c = slice((3 * which + 2) * D, (3 * which + 3) * D)
                for j in range(streams):
                    pool.dma_start(gates[:, j, :], mod_d[L.l, j:j + 1, c].to_broadcast([P, D])).then_inc(sem, 16)

            at(pool, *pr_b.done)
            pool.dma_start(cx, ins["ctx_2"][0].rearrange("(t p) d -> p t d", p=P)).then_inc(s_cx, 16)
            pool.dma_start(convrows, ins["conv_w_2"][0]).then_inc(s_conv.w_rows, 16)
            rope_loads(L0, "q_norm_a_2", "k_norm_a_2")
            pool_ffn(pool, f_b)

            at(pool, *f_b.mod_stored)
            for l in range(2):
                pool.dma_start(modrows[0:96, l, :], mod_d[l].rearrange("j (r c) -> (j r) c", c=P))\
                    .then_inc(s_mod.rows, 16)
            pool.wait_ge(s_glu.out, 4)
            pool.wait_ge(s_conv.w_ready, 1)
            at(pool, (used[T_ab[3].slot], T_ab[3].first + 1))
            for k in range(TAPS):
                for c in (2, 3):
                    if k == 0:
                        pool.tensor_scalar(conv[:, c], glu[:, c, :, 0:SEQ], convw[:, c, 0:1], vcol("conv_b_2", c),
                                           ALU.mult, ALU.add).then_inc(s_conv.taps_last, 1)
                        continue
                    pool.wait_ge(s_conv.product, 2 * (k - 1) + c - 1)
                    pool.wait_ge(s_conv.taps_last, 2 * (k - 1) + c - 1)
                    pool.tensor_tensor(conv[:, c], conv[:, c], tap_product(c, k), ALU.add)\
                        .then_inc(s_conv.taps_last, 1)
            at(pool, *L0.at.done)
            gate_loads(L0, 0, 2, L0.s.gate1)
            at(pool, *L0.pr.done)
            gate_loads(L0, 1, 2, L0.s.gate2)
            pool_moe(pool, moes[0])
            rope_loads(L1, "q_norm_c_2", "k_norm_c_2")
            at(pool, *moes[0].done)
            pool.dma_start(band.rearrange("p a b -> p (a b)"), ins["shape_window"].rearrange("p a b -> p (a b)"))\
                .then_inc(s_band.loaded, 16)
            pool.dma_start(pool_w, ins["pool_w_2"][0].rearrange("g c d -> c g d")).then_inc(s_band.weights, 16)
            pool.dma_start(sinks, ins["sink_c_2"][0:1, :].to_broadcast([P, 8])).then_inc(s_band.sinks, 16)
            at(pool, *L1.nc.read)
            pool.dma_start(pool_tab.rearrange("p a b c -> p (a b c)"), ins["shape_pool"]).then_inc(s_band.table, 16)
            at(pool, *L1.at.done)
            gate_loads(L1, 0, 1, L1.s.gate1)
            at(pool, *L1.pr.done)
            gate_loads(L1, 1, 1, L1.s.gate2)
            pool_moe(pool, moes[1])
            at(pool, *moes[1].done)
            pool.dma_start(out[0].rearrange("(t p) d -> p t d", p=P), hx[:, :, :]).then_inc(s_out, 16)
            pool.wait_ge(s_out, 16)



def kernel(**inputs):
    import concourse.bacc as bacc
    from concourse.bass_utils import run_bass_kernel_spmd as run

    nc = bacc.Bacc("TRN2", target_bir_lowering=False, num_devices=1)
    table, diag, rope, window, band = shape_constants()
    arrays = {name: np.ascontiguousarray(a) for name, a in inputs.items()}
    arrays.update(shape_table=table, shape_diag=diag, shape_rope=rope, shape_window=window, shape_pool=band)
    ins = {name: nc.dram_tensor(name, a.shape, mybir.dt.from_np(a.dtype), kind="ExternalInput").ap()
           for name, a in arrays.items()}
    out = nc.dram_tensor("out", (1, SEQ, D), F32, kind="ExternalOutput").ap()
    build(nc, ins, out)
    return run(nc, [arrays], core_ids=[0]).results[0]["out"]
```
